# Optimizing a Trainium2 kernel written in Bass

```python
import math
import jax, jax.numpy as jnp
from jax import lax
import numpy as np

D_MODEL = 1024
BATCH = 1
SEQ = 2048
DEPTH = 1

CHUNK = 64
HEAD_DIM = 64
SWA_HEADS = 8
SWA_KV_HEADS = 2
SWA_WINDOW = 128
SWA_CHUNKS = SWA_WINDOW // CHUNK
FOX_HEADS = 8
FOX_BLOCK = 128
D_FF = 4 * D_MODEL
EPS = 1e-6
NEG = -1e30

SWA_Q = SWA_HEADS * HEAD_DIM
SWA_KV = SWA_KV_HEADS * HEAD_DIM
FOX_W = FOX_HEADS * HEAD_DIM
D_MIX = SWA_Q + FOX_W
D_IN = SWA_Q + 2 * SWA_KV + 3 * FOX_W + FOX_HEADS

kernel_name = "hybrid_swa_sink_fox_sqrelu"

def rmsnorm(x, g):
    xf = x.astype(jnp.float32)
    xf = xf * lax.rsqrt(jnp.mean(xf * xf, axis=-1, keepdims=True) + EPS)
    return xf.astype(x.dtype) * g

def alibi_slopes(n_heads):
    return jnp.asarray(2.0 ** (-8.0 * np.arange(1, n_heads + 1) / n_heads), dtype=jnp.float32)

def swa_sink_attention(q, k, v, sinks):
    B, S = q.shape[0], q.shape[1]
    nc = S // CHUNK
    g = SWA_HEADS // SWA_KV_HEADS
    kb_len = SWA_CHUNKS * CHUNK
    qc = q.reshape(B, nc, CHUNK, SWA_KV_HEADS, g, HEAD_DIM)
    kc = k.reshape(B, nc, CHUNK, SWA_KV_HEADS, HEAD_DIM)
    vc = v.reshape(B, nc, CHUNK, SWA_KV_HEADS, HEAD_DIM)

    def band(a):
        pad = jnp.pad(a, ((0, 0), (SWA_CHUNKS - 1, 0), (0, 0), (0, 0), (0, 0)))
        return jnp.concatenate([pad[:, i:i + nc] for i in range(SWA_CHUNKS)], axis=2)

    kb, vb = band(kc), band(vc)
    scale = 1.0 / math.sqrt(HEAD_DIM)
    s = jnp.einsum('bnqhgd,bnkhd->bnhgqk', qc, kb).astype(jnp.float32) * scale

    q_pos = jnp.arange(nc)[:, None] * CHUNK + jnp.arange(CHUNK)[None, :]
    k_pos = (jnp.arange(nc)[:, None] - (SWA_CHUNKS - 1)) * CHUNK + jnp.arange(kb_len)[None, :]
    dist = jnp.abs(q_pos[:, :, None] - k_pos[:, None, :]).astype(jnp.float32)
    slopes = alibi_slopes(SWA_HEADS).reshape(SWA_KV_HEADS, g)
    s = s - slopes[None, None, :, :, None, None] * dist[None, :, None, None, :, :]
    s = jnp.where((k_pos >= 0)[None, :, None, None, None, :], s, NEG)

    sink = sinks.astype(jnp.float32).reshape(SWA_KV_HEADS, g)[None, None, :, :, None, None]
    m = jnp.maximum(jnp.max(s, axis=-1, keepdims=True), sink)
    p = jnp.exp(s - m)
    denom = jnp.sum(p, axis=-1, keepdims=True) + jnp.exp(sink - m)
    w = (p / denom).astype(v.dtype)
    out = jnp.einsum('bnhgqk,bnkhd->bnqhgd', w, vb)
    return out.reshape(B, S, SWA_Q)

def forgetting_attention(q, k, v, f_logit):
    B, S = q.shape[0], q.shape[1]
    nb = S // FOX_BLOCK
    scale = 1.0 / math.sqrt(HEAD_DIM)
    log_f = jax.nn.log_sigmoid(f_logit.astype(jnp.float32))
    c = jnp.cumsum(log_f, axis=1)
    c_keys = jnp.transpose(c, (0, 2, 1))
    qb = jnp.transpose(q.reshape(B, nb, FOX_BLOCK, FOX_HEADS, HEAD_DIM), (1, 0, 2, 3, 4))
    cb = jnp.transpose(c.reshape(B, nb, FOX_BLOCK, FOX_HEADS), (1, 0, 3, 2))
    k_pos = jnp.arange(S)

    def block(args):
        i, q_i, c_i = args
        s = jnp.einsum('bqhd,bkhd->bhqk', q_i, k).astype(jnp.float32) * scale
        s = s + c_i[..., None] - c_keys[:, :, None, :]
        q_pos = i * FOX_BLOCK + jnp.arange(FOX_BLOCK)
        s = jnp.where(k_pos[None, :] <= q_pos[:, None], s, NEG)
        p = jax.nn.softmax(s, axis=-1).astype(v.dtype)
        return jnp.einsum('bhqk,bkhd->bqhd', p, v)

    out = lax.map(block, (jnp.arange(nb), qb, cb))
    return jnp.transpose(out, (1, 0, 2, 3, 4)).reshape(B, S, FOX_W)

def setup_inputs(seed: int = 0) -> dict:
    key = jax.random.key(seed)
    ks = jax.random.split(key, 12)
    f32 = jnp.float32
    x = jax.random.normal(ks[0], (BATCH, SEQ, D_MODEL), f32)
    norm_mix = 1.0 + 0.02 * jax.random.normal(ks[1], (DEPTH, D_MODEL), f32)
    w_in = jax.random.normal(ks[2], (DEPTH, D_MODEL, D_IN), f32) * D_MODEL ** -0.5
    b_forget = 3.0 + 0.5 * jax.random.normal(ks[3], (DEPTH, FOX_HEADS), f32)
    sinks = 0.5 * jax.random.normal(ks[4], (DEPTH, SWA_HEADS), f32)
    w_out = jax.random.normal(ks[5], (DEPTH, D_MIX, D_MODEL), f32) * D_MIX ** -0.5
    norm_mlp = 1.0 + 0.02 * jax.random.normal(ks[6], (DEPTH, D_MODEL), f32)
    w_up = jax.random.normal(ks[7], (DEPTH, D_MODEL, D_FF), f32) * D_MODEL ** -0.5
    w_down = jax.random.normal(ks[8], (DEPTH, D_FF, D_MODEL), f32) * D_FF ** -0.5
    norm_final = 1.0 + 0.02 * jax.random.normal(ks[9], (D_MODEL,), f32)
    return {"x": x, "norm_mix": norm_mix, "w_in": w_in, "b_forget": b_forget,
            "sinks": sinks, "w_out": w_out, "norm_mlp": norm_mlp, "w_up": w_up,
            "w_down": w_down, "norm_final": norm_final}

def reference(x, norm_mix, w_in, b_forget, sinks, w_out, norm_mlp, w_up, w_down, norm_final):
    B, S = x.shape[0], x.shape[1]
    o1 = SWA_Q
    o2 = o1 + SWA_KV
    o3 = o2 + SWA_KV
    o4 = o3 + FOX_W
    o5 = o4 + FOX_W
    o6 = o5 + FOX_W
    for l in range(DEPTH):
        h = rmsnorm(x, norm_mix[l])
        proj = jnp.einsum('bsd,de->bse', h, w_in[l])
        qa = proj[..., :o1].reshape(B, S, SWA_HEADS, HEAD_DIM)
        ka = proj[..., o1:o2].reshape(B, S, SWA_KV_HEADS, HEAD_DIM)
        va = proj[..., o2:o3].reshape(B, S, SWA_KV_HEADS, HEAD_DIM)
        qb = proj[..., o3:o4].reshape(B, S, FOX_HEADS, HEAD_DIM)
        kb = proj[..., o4:o5].reshape(B, S, FOX_HEADS, HEAD_DIM)
        vb = proj[..., o5:o6].reshape(B, S, FOX_HEADS, HEAD_DIM)
        f_logit = proj[..., o6:] + b_forget[l]
        out_a = swa_sink_attention(qa, ka, va, sinks[l])
        out_b = forgetting_attention(qb, kb, vb, f_logit)
        mixed = jnp.concatenate([out_a, out_b], axis=-1)
        x = x + jnp.einsum('bse,ed->bsd', mixed, w_out[l])
        h = rmsnorm(x, norm_mlp[l])
        u = jax.nn.relu(jnp.einsum('bsd,df->bsf', h, w_up[l]))
        x = x + jnp.einsum('bsf,fd->bsd', u * u, w_down[l])
    return rmsnorm(x, norm_final)


_drawn_inputs = setup_inputs


def setup_inputs(seed=0):
    import zlib

    import numpy as np

    out = dict(_drawn_inputs(seed))
    spreads = {}
    factors = {'norm_mix': 5.817, 'sinks': 8.0, 'norm_mlp': 3.1, 'norm_final': 2.848}
    for name, (base, spread) in spreads.items():
        noise = np.random.default_rng([zlib.crc32(name.encode()), seed]).standard_normal(out[name].shape)
        drawn = base * np.exp(spread * noise) if base else spread * noise
        out[name] = __import__('jax').numpy.asarray(drawn.astype(out[name].dtype))
    for name, factor in factors.items():
        out[name] = (out[name] * factor).astype(out[name].dtype)
    return out
```

```python
from contextlib import ExitStack

import concourse.bass as bass
from concourse import mybir

F32 = mybir.dt.float32
F32R = mybir.dt.float32r
ALU = mybir.AluOpType
ACT = mybir.ActivationFunctionType

P = 128
EPS = 1e-6
CHUNK = 64
HEAD_DIM = 64
SWA_HEADS = 8
SWA_KV_HEADS = 2
FOX_HEADS = 8
NEG = -1e30
BANK = 512


def scopes(nc, ctx):
    def sb(name, shape, dt=F32):
        return ctx.enter_context(nc.sbuf_tensor(name, shape, dt))

    def pb(name, n=BANK, rows=P):
        return ctx.enter_context(nc.psum_tensor(name, [rows, n], F32))

    def sem(name):
        return ctx.enter_context(nc.semaphore(name))

    return sb, pb, sem


def project(nc, x, norm_mix, w_in, ident_dram, proj_hi, proj_lo):
    S, D = x.shape
    DK = D // P
    ST = S // P
    SB = S // BANK
    TPB = ST // SB
    N_IN = w_in.shape[1]
    NCH = -(-N_IN // P)
    LAST = N_IN - P
    with ExitStack() as ctx:
        sb, pb, sem = scopes(nc, ctx)
        ident = sb("p_ident", [P, P])
        gain = sb("p_gain", [P, D])
        mhalf = sb("p_mhalf", [P, 1])
        x_in = sb("p_x_in", [P, 2, D])
        ssum = sb("p_ssum", [P, ST])
        rstd = sb("p_rstd", [P, ST])
        xn = sb("p_xn", [P, 2, D])
        ht_hi = sb("p_ht_hi", [P, DK, S], F32R)
        ht_lo = sb("p_ht_lo", [P, DK, S], F32R)
        w_raw = sb("p_w_raw", [P, 2, DK, P])
        w_hi = sb("p_w_hi", [P, 2, DK, P], F32R)
        w_lo = sb("p_w_lo", [P, 2, DK, P], F32R)
        o_hi = sb("p_o_hi", [P, 2, S], F32R)
        o_lo = sb("p_o_lo", [P, 2, S], F32R)
        ps_t = [pb(f"p_ps_t{i}") for i in range(4)]
        ps_o = [pb(f"p_ps_o{i}") for i in range(4)]

        const_in = sem("p_const_in")
        x_loaded = [sem(f"p_x_loaded{i}") for i in range(2)]
        w_loaded = [sem(f"p_w_loaded{i}") for i in range(2)]
        mhalf_set = sem("p_mhalf_set")
        squared = sem("p_squared")
        meaned = sem("p_meaned")
        rooted = sem("p_rooted")
        normed = sem("p_normed")
        turned = sem("p_turned")
        ht_hi_done = sem("p_ht_hi_done")
        ht_lo_done = sem("p_ht_lo_done")
        w_hi_done = sem("p_w_hi_done")
        w_lo_done = sem("p_w_lo_done")
        summed = sem("p_summed")
        o_hi_done = sem("p_o_hi_done")
        o_lo_done = sem("p_o_lo_done")
        stored = [sem(f"p_stored{i}") for i in range(2)]

        x_tiles = x.rearrange("(t p) d -> t p d", p=P)
        w_v = w_in.rearrange("(k p) n -> p k n", p=P)
        block = ctx.enter_context(nc.Block())

        PAIRS = NCH // 2
        assert NCH == 2 * PAIRS + 1 and LAST > (NCH - 2) * P

        @block.sync
        def _(sp):
            def load_weights(pair, slot, col):
                if not isinstance(pair, int) or pair >= 1:
                    sp.wait_ge(w_lo_done, 2 * pair + slot - 1)
                sp.dma_start(w_raw[:, slot], w_v[:, :, bass.ds(col, P)]).then_inc(w_loaded[slot], 16)

            def store(pair, slot):
                n = 2 * pair + slot
                sp.wait_ge(o_lo_done, 2 * SB if isinstance(pair, int) and pair == 0 else (n + 1) * SB)
                sp.dma_start(proj_hi[bass.ds(n * P, P), :], o_hi[:, slot].bitcast(F32)).then_inc(stored[slot], 16)
                sp.dma_start(proj_lo[bass.ds(n * P, P), :], o_lo[:, slot].bitcast(F32)).then_inc(stored[slot], 16)

            sp.dma_start(x_in[:, 0], x_tiles[0]).then_inc(x_loaded[0], 16)
            sp.dma_start(gain[:], norm_mix[0].partition_broadcast(P)).then_inc(const_in, 16)
            sp.dma_start(ident[:], ident_dram).then_inc(const_in, 16)
            sp.dma_start(x_in[:, 1], x_tiles[1]).then_inc(x_loaded[1], 16)
            for slot in range(2):
                load_weights(0, slot, slot * P)
            for t in range(2, ST):
                sp.wait_ge(normed, t - 1)
                sp.dma_start(x_in[:, t % 2], x_tiles[t]).then_inc(x_loaded[t % 2], 16)
            for slot in range(2):
                load_weights(1, slot, (2 + slot) * P)
            for slot in range(2):
                store(0, slot)
            with sp.Fori(1, PAIRS - 1) as i:
                for slot in range(2):
                    load_weights(i + 1, slot, (2 * i + 2 + slot) * P)
                    store(i, slot)
            load_weights(PAIRS, 0, LAST)
            store(PAIRS - 1, 0)
            store(PAIRS - 1, 1)
            store(PAIRS, 0)
            for slot in range(2):
                sp.wait_ge(stored[slot], 32 * (PAIRS + 1 - slot))

        @block.gpsimd
        def _(pool):
            for t in range(ST):
                pool.wait_ge(squared, t + 1)
                nc.gpsimd.tensor_scalar(rstd[:, t:t + 1], ssum[:, t:t + 1], 1.0 / D, EPS,
                                        ALU.mult, ALU.add).then_inc(meaned, 1)
                pool.wait_ge(meaned, t + 1)
                if t == 0:
                    pool.wait_ge(mhalf_set, 1)
                nc.gpsimd.tensor_tensor(rstd[:, t:t + 1], rstd[:, t:t + 1], mhalf[:],
                                        ALU.pow).then_inc(rooted, 1)

        @block.scalar
        def _(act):
            def square(t):
                act.wait_ge(x_loaded[t % 2], 16 * (t // 2 + 1))
                if t >= 2:
                    act.wait_ge(turned, 2 * (t - 1))
                nc.scalar.activation(xn[:, t % 2], x_in[:, t % 2], ACT.Square,
                                     accum_out=ssum[:, t:t + 1]).then_inc(squared, 1)

            def split_ht_hi(t):
                for half in range(2):
                    act.wait_ge(turned, 2 * t + half + 1)
                    nc.scalar.activation(
                        ht_hi[:, 4 * half:4 * half + 4, t * P:(t + 1) * P],
                        ps_t[2 * (t % 2) + half][:].rearrange("p (k s) -> p k s", s=P),
                        ACT.Copy).then_inc(ht_hi_done, 1)

            def split_w_hi(pair, slot):
                act.wait_ge(w_loaded[slot], 16 * (pair + 1))
                if not isinstance(pair, int) or pair >= 1:
                    act.wait_ge(summed, (2 * pair + slot - 1) * SB)
                nc.scalar.activation(w_hi[:, slot], w_raw[:, slot], ACT.Copy).then_inc(w_hi_done, 1)

            def split_o_hi(slot, b, bank, count):
                act.wait_ge(summed, count + 1)
                nc.scalar.activation(o_hi[:, slot, b * BANK:(b + 1) * BANK], ps_o[bank][:],
                                     ACT.Copy).then_inc(o_hi_done, 1)

            square(0)
            split_w_hi(0, 0)
            split_w_hi(0, 1)
            for t in range(ST):
                if t + 1 < ST:
                    square(t + 1)
                split_ht_hi(t)
                if t % TPB == TPB - 1 and t // TPB >= 1:
                    b = t // TPB - 1
                    for slot in range(2):
                        split_o_hi(slot, b, (2 * b + slot) % 4, 2 * b + slot)
            split_o_hi(0, SB - 1, 2, 2 * SB - 2)
            split_o_hi(1, SB - 1, 3, 2 * SB - 1)
            split_w_hi(1, 0)

            def chunk(pair, slot, last=False):
                act.wait_ge(stored[slot], 32 * pair)
                for b in range(SB):
                    split_o_hi(slot, b, b, (2 * pair + slot) * SB + b)
                    if b == 0 and not last:
                        split_w_hi(pair + slot, 1 - slot)

            with act.Fori(1, PAIRS - 1) as i:
                chunk(i, 0)
                chunk(i, 1)
            chunk(PAIRS - 1, 0)
            chunk(PAIRS - 1, 1)
            chunk(PAIRS, 0, True)

        @block.vector
        def _(dve):
            def norm(t):
                dve.wait_ge(rooted, t + 1)
                if t == 0:
                    dve.wait_ge(const_in, 32)
                nc.vector.scalar_tensor_tensor(xn[:, t % 2], x_in[:, t % 2], rstd[:, t:t + 1], gain[:],
                                               ALU.mult, ALU.mult).then_inc(normed, 1)

            def split_ht_lo(t):
                for half in range(2):
                    dve.wait_ge(ht_hi_done, 2 * t + half + 1)
                    k, s = slice(4 * half, 4 * half + 4), slice(t * P, (t + 1) * P)
                    nc.vector.tensor_tensor(
                        ht_lo[:, k, s], ps_t[2 * (t % 2) + half][:].rearrange("p (k s) -> p k s", s=P),
                        ht_hi[:, k, s].bitcast(F32), ALU.subtract).then_inc(ht_lo_done, 1)

            def split_w_lo(n, slot=None):
                slot = n if slot is None else slot
                dve.wait_ge(w_hi_done, n + 1)
                nc.vector.tensor_tensor(w_lo[:, slot], w_raw[:, slot], w_hi[:, slot].bitcast(F32),
                                        ALU.subtract).then_inc(w_lo_done, 1)

            def split_o_lo(slot, b, bank, count):
                dve.wait_ge(o_hi_done, count + 1)
                s = slice(b * BANK, (b + 1) * BANK)
                nc.vector.tensor_tensor(o_lo[:, slot, s], ps_o[bank][:], o_hi[:, slot, s].bitcast(F32),
                                        ALU.subtract).then_inc(o_lo_done, 1)

            nc.vector.memset(mhalf[:], -0.5).then_inc(mhalf_set, 1)
            norm(0)
            split_w_lo(0)
            split_w_lo(1)
            for t in range(ST):
                if t + 1 < ST:
                    norm(t + 1)
                split_ht_lo(t)
                if t % TPB == TPB - 1 and t // TPB >= 1:
                    b = t // TPB - 1
                    for slot in range(2):
                        split_o_lo(slot, b, (2 * b + slot) % 4, 2 * b + slot)
            split_o_lo(0, SB - 1, 2, 2 * SB - 2)
            split_o_lo(1, SB - 1, 3, 2 * SB - 1)
            split_w_lo(2, 0)

            def chunk(pair, slot, last=False):
                n = 2 * pair + slot
                for b in range(SB):
                    split_o_lo(slot, b, b, n * SB + b)
                    if b == 0 and not last:
                        split_w_lo(n + 1, 1 - slot)

            with dve.Fori(1, PAIRS - 1) as i:
                chunk(i, 0)
                chunk(i, 1)
            chunk(PAIRS - 1, 0)
            chunk(PAIRS - 1, 1)
            chunk(PAIRS, 0, True)

        @block.tensor
        def _(pe):
            def turn(t):
                pe.wait_ge(normed, t + 1)
                if t == 0:
                    pe.wait_ge(const_in, 32)
                if t >= 2:
                    pe.wait_ge(ht_lo_done, 2 * (t - 1))
                for half in range(2):
                    for k in range(4):
                        last = nc.tensor.transpose(ps_t[2 * (t % 2) + half][:, k * P:(k + 1) * P],
                                                   xn[:, t % 2, (4 * half + k) * P:(4 * half + k + 1) * P],
                                                   ident[:])
                    last.then_inc(turned, 1)

            def product(slot, b, bank):
                s = slice(b * BANK, (b + 1) * BANK)
                for k in range(DK):
                    for n, (w, h) in enumerate(((w_hi, ht_hi), (w_hi, ht_lo), (w_lo, ht_hi))):
                        last = nc.tensor.matmul(ps_o[bank][:], w[:, slot, k, :], h[:, k, s],
                                                start=(k == 0 and n == 0), stop=(k == DK - 1 and n == 2))
                last.then_inc(summed, 1)

            for b in range(SB + 1):
                if b < SB:
                    for t in range(b * TPB, (b + 1) * TPB):
                        turn(t)
                if b >= 1:
                    pe.wait_ge(ht_lo_done, 2 * TPB * b)
                    pe.wait_ge(w_lo_done, 2)
                    for slot in range(2):
                        n = 2 * (b - 1) + slot
                        if n >= 4:
                            pe.wait_ge(o_lo_done, n - 3)
                        product(slot, b - 1, n % 4)

            def chunk(pair, slot):
                n = 2 * pair + slot
                pe.wait_ge(w_lo_done, n + 1)
                for b in range(SB):
                    pe.wait_ge(o_lo_done, n * SB + b - 3)
                    product(slot, b, b)

            with pe.Fori(1, PAIRS - 1) as i:
                chunk(i, 0)
                chunk(i, 1)
            chunk(PAIRS - 1, 0)
            chunk(PAIRS - 1, 1)
            chunk(PAIRS, 0)


FLT_MAX = 3.4028234e38


def gate(nc, proj_hi, proj_lo, b_forget, decay):
    S = proj_hi.shape[1]
    G = FOX_HEADS
    row = proj_hi.shape[0] - G
    with ExitStack() as ctx:
        sb, pb, sem = scopes(nc, ctx)
        f = sb("g_f", [G, S])
        f_lo = sb("g_f_lo", [G, S])
        bias = sb("g_bias", [G, 1])
        ones = sb("g_ones", [G, S])
        mag = sb("g_mag", [G, S])
        e = sb("g_e", [G, S])
        c = sb("g_c", [G, S])
        loaded = sem("g_loaded")
        step = sem("g_step")
        mag_done = sem("g_mag_done")
        log_done = sem("g_log_done")
        stored = sem("g_stored")
        block = ctx.enter_context(nc.Block())

        @block.sync
        def _(sp):
            sp.dma_start(f[:], proj_hi[row:row + G, :]).then_inc(loaded, 16)
            sp.dma_start(f_lo[:], proj_lo[row:row + G, :]).then_inc(loaded, 16)
            sp.dma_start(bias[:], b_forget.rearrange("a g -> g a")).then_inc(loaded, 16)
            sp.wait_ge(step, 7)
            sp.dma_start(decay, c[:]).then_inc(stored, 16)
            sp.wait_ge(stored, 16)

        @block.vector
        def _(dve):
            nc.vector.memset(ones[:], 1.0).then_inc(step, 1)
            dve.wait_ge(loaded, 48)
            nc.vector.tensor_tensor(f[:], f[:], f_lo[:], ALU.add).then_inc(step, 1)
            dve.wait_ge(step, 2)
            nc.vector.tensor_scalar(f[:], f[:], bias[:], None, ALU.add).then_inc(step, 1)
            dve.wait_ge(step, 3)
            nc.vector.tensor_scalar(f_lo[:], f[:], -1.0, 0.0, ALU.mult, ALU.max).then_inc(step, 1)
            dve.wait_ge(log_done, 1)
            dve.wait_ge(step, 4)
            nc.vector.tensor_tensor(e[:], e[:], f_lo[:], ALU.add).then_inc(step, 1)
            dve.wait_ge(step, 5)
            nc.vector.tensor_tensor_scan(c[:], ones[:], e[:], 0.0, ALU.mult, ALU.add).then_inc(step, 1)
            dve.wait_ge(step, 6)
            nc.vector.tensor_scalar(c[:], c[:], float(HEAD_DIM) ** 0.5, None, ALU.mult).then_inc(step, 1)

        @block.scalar
        def _(act):
            act.wait_ge(step, 3)
            nc.scalar.activation(mag[:], f[:], ACT.Abs).then_inc(mag_done, 1)
            act.wait_ge(mag_done, 1)
            nc.scalar.activation(e[:], mag[:], ACT.Exp, scale=-1.0).then_inc(mag_done, 1)
            act.wait_ge(mag_done, 2)
            nc.scalar.activation(e[:], e[:], ACT.Ln, bias=1.0).then_inc(log_done, 1)


def attend(nc, proj_hi, proj_lo, sinks, ident_dram, causal_dram, alibi_dram,
           decay, o_main, o_rest, rsum_inv):
    S = proj_hi.shape[1]
    QT = S // P
    QB = QT // 4
    DH = HEAD_DIM
    H = SWA_HEADS
    GROUP = SWA_HEADS // SWA_KV_HEADS
    KA = SWA_HEADS * DH
    VA = KA + SWA_KV_HEADS * DH
    QF = VA + SWA_KV_HEADS * DH
    KF = QF + FOX_HEADS * DH
    VF = KF + FOX_HEADS * DH
    GATE = -(-(VF + FOX_HEADS * DH) // P) * P + P - FOX_HEADS
    SCALE = float(DH) ** -0.5
    assert SWA_HEADS == FOX_HEADS and QB == 4 and 2 * DH == P

    steps = [("swa", j) for j in range(QT // 2)] + [("fox", b, k) for b in range(QB) for k in range(4 * b + 4)]
    NSTEP = len(steps)
    BLOCK0 = [QT // 2 + 4 * (b * (b + 1) // 2) for b in range(QB)]
    fox_chunks = [[("fox", b, t, c) for t in range(4) for c in range(b + 1)] for b in range(QB)]
    swa_chunks = [("swa", j) for j in range(QT // 2)]
    chunk_at = [[] for _ in range(NSTEP)]
    for n, c in enumerate(fox_chunks[0] + fox_chunks[1]):
        chunk_at[n // 2 if n < 8 else n - 4].append(c)
    for n, c in enumerate(fox_chunks[2]):
        chunk_at[8 + (n // 2 if n < 8 else n - 4)].append(c)
    for n, c in enumerate(fox_chunks[3]):
        chunk_at[18 + (n // 2 if n < 12 else n - 6)].append(c)
    for n, c in enumerate(swa_chunks):
        chunk_at[30 + 3 * n // 2].append(("next",) + c)
    turn_at = [[] for _ in range(NSTEP)]
    for g in range(4):
        turn_at[g].append(("v", "fox", g))
        turn_at[34 + g].append(("v", "swa", g))
    turn_at[38].append(("r",))
    for i in range(NSTEP):
        turn_at[i].append(("p", (i + 2) % NSTEP) if i + 2 < NSTEP else ("next", "p", i + 2 - NSTEP))
    NCHUNK = len(swa_chunks) + sum(map(len, fox_chunks))
    NTURN = sum(map(len, turn_at))
    S_RING, T_RING, PT_RING, O_RING = 3, 3, 4, 4
    assert NCHUNK % S_RING == 0 and NTURN % T_RING == 0 and NSTEP % PT_RING == 0
    PRE_CHUNKS = len(swa_chunks)
    PRE_TURNS = [("v", "swa", g) for g in range(4)] + [("next", "p", 0), ("next", "p", 1)]
    turn_order = [g for at in turn_at for g in at]
    last_order = [g for g in turn_order if g[0] != "next" and g[:2] != ("v", "swa")]
    assert len(PRE_TURNS) % T_RING == 0
    BEFORE = -1

    def p_slot(kind, b=0):
        if kind == "swa":
            return 0, 0
        return (1, 1, 0, 1)[b], (0, 4 * BANK, 0, 0)[b]

    def width(b, t, c):
        return BANK if c < b else (t + 1) * P

    with ExitStack() as ctx:
        sb, pb, sem = scopes(nc, ctx)
        ident = sb("a_ident", [P, P])
        ident_r = sb("a_ident_r", [P, P], F32R)
        causal = sb("a_causal", [P, P])
        causal_r = sb("a_causal_r", [P, P], F32R)
        q_st = {k: sb(f"a_q_{k}", [P, S], F32R) for k in ("swa", "fox")}
        k_hi = {k: sb(f"a_k_hi_{k}", [P, S], F32R) for k in ("swa", "fox")}
        k_lo = {k: sb(f"a_k_lo_{k}", [P, S], F32R) for k in ("swa", "fox")}
        v_t = {k: sb(f"a_v_t_{k}", [P, S]) for k in ("swa", "fox")}
        v_st = {k: sb(f"a_v_{k}", [P, QT, P], F32R) for k in ("swa", "fox")}
        alibi = sb("a_alibi", [P, 2 * P])
        sink = sb("a_sink", [P, 1])
        sink_neg = sb("a_sink_neg", [P, 1])
        decay_sb = sb("a_decay", [P, S])
        probs = [sb(f"a_probs{i}", [P, 4 * S]) for i in range(2)]
        neg_max = {"swa": sb("a_nm_swa", [P, QT]), "fox": sb("a_nm_fox", [P, QT, 4])}
        rsum = {k: sb(f"a_rsum_{k}", [P, QT]) for k in ("swa", "fox")}
        sink_exp = sb("a_sink_exp", [P, QT])
        recip = sb("a_recip", [P, 2 * QT])
        recip_t = sb("a_recip_t", [2 * QT, P])
        pt_hi = [sb(f"a_pt_hi{i}", [P, BANK], F32R) for i in range(PT_RING)]
        pt_lo = [sb(f"a_pt_lo{i}", [P, BANK], F32R) for i in range(PT_RING)]
        o_sb = [sb(f"a_o{i}", [P, BANK]) for i in range(O_RING)]
        ps_s = [pb(f"a_ps_s{i}") for i in range(S_RING)]
        ps_t = [pb(f"a_ps_t{i}") for i in range(T_RING)]
        ps_o = [pb(f"a_ps_o{i}") for i in range(2)]

        const_in = sem("a_const_in")
        const_r = sem("a_const_r")
        qk_loaded = {k: sem(f"a_qk_loaded_{k}") for k in ("swa", "fox")}
        v_loaded = {k: sem(f"a_v_loaded_{k}") for k in ("swa", "fox")}
        sink_negated = sem("a_sink_negated")
        summed = sem("a_summed")
        scored = sem("a_scored")
        exped = sem("a_exped")
        turned = sem("a_turned")
        p_hi_done = sem("a_p_hi_done")
        p_lo_done = sem("a_p_lo_done")
        v_done = {k: sem(f"a_v_done_{k}") for k in ("swa", "fox")}
        weighted = sem("a_weighted")
        o_copied = sem("a_o_copied")
        o_stored = [sem(f"a_o_stored{i}") for i in range(O_RING)]
        sink_exped = sem("a_sink_exped")
        denom_done = sem("a_denom_done")
        recip_done = sem("a_recip_done")
        r_copied = sem("a_r_copied")
        r_stored = sem("a_r_stored")

        chunk_no, tile_no = {}, {}
        for i in range(NSTEP):
            for c in chunk_at[i]:
                chunk_no[c] = len(chunk_no)
                if c[0] == "fox" and c[3] == c[1]:
                    tile_no[("fox", c[1], c[2])] = len(tile_no)
                elif c[0] == "next":
                    tile_no[("next", "swa", 2 * c[2])] = len(tile_no)
                    tile_no[("next", "swa", 2 * c[2] + 1)] = len(tile_no)
        NTILE = len(tile_no)
        PRE_TILES = QT

        def chunk_count(h, c):
            n = chunk_no[c] if c in chunk_no else chunk_no[("next",) + c] - NCHUNK
            return h * NCHUNK + (PRE_CHUNKS + n + 1)

        def tile_count(h, t):
            n = tile_no[t] if t in tile_no else tile_no[("next",) + t] - NTILE
            return h * NTILE + (PRE_TILES + n + 1)

        def order_of(h):
            if isinstance(h, int) and h in (BEFORE, H - 1):
                return PRE_TURNS if h == BEFORE else last_order
            return turn_order

        def turn_count(h, g):
            before = 0 if h is BEFORE else h * NTURN + len(PRE_TURNS)
            return before + (order_of(h).index(g) + 1)

        def chunk_ring(c):
            n = chunk_no[c] if c in chunk_no else chunk_no[("next",) + c] - NCHUNK
            return (PRE_CHUNKS + n) % S_RING

        O_BLOCKS = 2 * QB

        def o_block(step):
            if step[0] == "swa":
                return step[1] // 2, step[1] % 2 == 0, step[1] % 2 == 1
            return QB + step[1], step[2] == 0, step[2] == 4 * step[1] + 3

        def p_cols(b, t, lo, hi):
            slot, at = p_slot("fox", b)
            row = at + t * BANK * (b + 1)
            return probs[slot][:, row + lo:row + hi]

        def swa_cols(t, lo, hi):
            return probs[0][:, t * 2 * P + lo:t * 2 * P + hi]

        def turn_width(step):
            if step[0] == "swa":
                return BANK
            return (4 - max(0, step[2] - 4 * step[1])) * P

        def turned_cols(i):
            if steps[i][0] == "swa":
                return (0 if i else P), BANK
            return 0, turn_width(steps[i])

        block = ctx.enter_context(nc.Block())

        @block.sync
        def _(sp):
            def load(dst, src, done):
                sp.dma_start(dst, src).then_inc(done, 16)

            def load_head(kind, q0, k0, v0):
                for part, half in ((0, proj_hi), (1, proj_lo)):
                    rows = slice(part * DH, (part + 1) * DH)
                    load(q_st[kind][rows].bitcast(F32), half[bass.ds(q0, DH), :], qk_loaded[kind])
                    for dst, src in ((k_hi, proj_hi), (k_lo, proj_lo)):
                        load(dst[kind][rows].bitcast(F32), src[bass.ds(k0, DH), :], qk_loaded[kind])
                    load(v_t[kind][rows], half[bass.ds(v0, DH), :], v_loaded[kind])

            def load_swa(h):
                load_head("swa", h * DH, KA + (h // GROUP) * DH, VA + (h // GROUP) * DH)
                load(alibi[:], alibi_dram[bass.ds(h, 1)].rearrange("a p c -> (a p) c"), qk_loaded["swa"])
                load(sink[:], sinks[0, bass.ds(h, 1)].partition_broadcast(P), qk_loaded["swa"])

            def load_fox(h):
                load_head("fox", QF + h * DH, KF + h * DH, VF + h * DH)
                load(decay_sb[:], decay[bass.ds(h, 1)].rearrange("a s -> (a s)").partition_broadcast(P),
                     qk_loaded["fox"])

            for done in (*o_stored, r_stored):
                sp.sem_inc(done, 16)
            load(ident[:], ident_dram, const_in)
            load(causal[:], causal_dram, const_in)
            load_swa(0)
            load_fox(0)

            def store_outputs(h, n):
                sp.wait_ge(o_copied, h * O_BLOCKS + (n + 3))
                row = (n // QB) * KA + h * DH
                cols = slice((n % QB) * BANK, (n % QB + 1) * BANK)
                for part, dst in ((0, o_main), (1, o_rest)):
                    load(dst[bass.ds(row, DH), cols], o_sb[n % O_RING][part * DH:(part + 1) * DH], o_stored[n % O_RING])

            def turn(h, last=False):
                if not last:
                    sp.wait_ge(scored, chunk_count(h, ("swa", QT // 2 - 1)))
                    sp.wait_ge(v_done["swa"], 4 * (h + 1))
                    sp.wait_ge(sink_exped, h + 1)
                    load_swa(h + 1)
                for n in range(QB + 2):
                    store_outputs(h, n)
                if not last:
                    sp.wait_ge(scored, chunk_count(h, ("fox", 3, 3, 3)))
                    sp.wait_ge(v_done["fox"], 4 * (h + 1))
                    load_fox(h + 1)
                store_outputs(h, QB + 2)
                sp.wait_ge(r_copied, h + 2)
                for part in range(2):
                    load(rsum_inv[bass.ds(part * H + h, 1)].rearrange("a (t q) -> (a t) q", q=P),
                         recip_t[part * QT:(part + 1) * QT], r_stored)
                store_outputs(h, QB + 3)

            with sp.Fori(0, H - 1) as h:
                turn(h)
            turn(H - 1, True)
            for done in o_stored:
                sp.wait_ge(done, 16 + 32 * H * O_BLOCKS // O_RING)
            sp.wait_ge(r_stored, 16 + 32 * H)

        @block.tensor
        def _(pe):
            def scores(h, c):
                ring = chunk_ring(c)
                if not (h is BEFORE and c[2] < S_RING):
                    pe.wait_ge(scored, chunk_count(h, c) - S_RING)
                kind = c[1] if c[0] == "next" else c[0]
                if kind == "swa":
                    j = c[2]
                    if j == 0:
                        pe.wait_ge(qk_loaded["swa"], (h + 1) * 128 + 128)
                    for n in range(2):
                        t = 2 * j + n
                        lo = 0 if t else P
                        out = ps_s[ring][:, n * 2 * P + lo:(n + 1) * 2 * P]
                        for m, kk in enumerate((k_hi, k_lo)):
                            last = nc.tensor.matmul(out, q_st[kind][:, t * P:(t + 1) * P],
                                                    kk[kind][:, (t - 1) * P + lo:(t + 1) * P],
                                                    start=(m == 0), stop=(m == 1))
                else:
                    _, b, t, n = c
                    if (b, t, n) == (0, 0, 0):
                        pe.wait_ge(qk_loaded["fox"], h * 112 + 112)
                        if isinstance(h, int) and h == 0:
                            pe.wait_ge(const_r, 2)
                    w = width(b, t, n)
                    q = slice((4 * b + t) * P, (4 * b + t + 1) * P)
                    for m, kk in enumerate((k_hi, k_lo)):
                        last = nc.tensor.matmul(ps_s[ring][:, 0:w], q_st[kind][:, q],
                                                kk[kind][:, n * BANK:n * BANK + w],
                                                start=(m == 0), stop=(m == 1 and n < b))
                    if n == b:
                        last = nc.tensor.matmul(ps_s[ring][:, w - P:w], ident_r[:], causal_r[:],
                                                start=False, stop=True)
                last.then_inc(summed, 1)

            def wait_bank_read(h, g):
                what = g[1:] if g[0] == "next" else g
                if what[0] == "v":
                    head = h + 1 if what[1] == "swa" else h
                    pe.wait_ge(v_done[what[1]], 4 * head + what[2] + 1)
                elif what[0] == "r":
                    pe.wait_ge(r_copied, h + 2)
                else:
                    head = h + 1 if g[0] == "next" else h
                    pe.wait_ge(p_lo_done, head * NSTEP + what[1] + 2)

            def turn_over(h, g):
                order = order_of(h)
                n = order.index(g)
                ring = n % T_RING
                if n >= T_RING:
                    wait_bank_read(h, order[n - T_RING])
                elif h is not BEFORE:
                    wait_bank_read(h - 1, turn_order[n - T_RING])
                    if n == 0:
                        pe.wait_ge(v_done["swa"], 4 * h + 4)
                what = g[1:] if g[0] == "next" else g
                bank = ps_t[ring]
                if what[0] == "v":
                    kind = what[1]
                    if what[2] == 0:
                        pe.wait_ge(v_loaded[kind], 32 * ((h + 1 if kind == "swa" else h) + 1))
                        if h is BEFORE:
                            pe.wait_ge(const_in, 32)
                    for m in range(4):
                        k = 4 * what[2] + m
                        last = nc.tensor.transpose(bank[:, m * P:(m + 1) * P],
                                                   v_t[kind][:, k * P:(k + 1) * P], ident[:])
                elif what[0] == "r":
                    pe.wait_ge(recip_done, 2 * h + 3)
                    last = nc.tensor.transpose(bank[0:2 * QT, 0:P], recip[:], ident[:])
                else:
                    step = steps[what[1]]
                    if step[0] == "swa":
                        j = step[1]
                        pe.wait_ge(exped, tile_count(h + 1 if g[0] == "next" else h, ("swa", 2 * j + 1)))
                        for m, (q, half) in enumerate(((2 * j, 0), (2 * j, 1), (2 * j + 1, 0), (2 * j + 1, 1))):
                            if (q, half) == (0, 0):
                                continue
                            last = nc.tensor.transpose(bank[:, m * P:(m + 1) * P],
                                                       swa_cols(q, half * P, (half + 1) * P), ident[:])
                    else:
                        _, b, k = step
                        if k == 0:
                            pe.wait_ge(exped, tile_count(h, ("fox", b, 3)))
                        first = max(0, k - 4 * b)
                        for m, t in enumerate(range(first, 4)):
                            last = nc.tensor.transpose(bank[:, m * P:(m + 1) * P],
                                                       p_cols(b, t, k * P, (k + 1) * P), ident[:])
                last.then_inc(turned, 1)

            def weigh(h, i):
                step = steps[i]
                kind = step[0]
                n, first, last_one = o_block(step)
                pe.wait_ge(p_lo_done, h * NSTEP + i + 2)
                if kind == "swa" and i == 0:
                    pe.wait_ge(v_done["swa"], h * 4 + 4)
                if kind == "fox" and i == BLOCK0[0]:
                    pe.wait_ge(v_done["fox"], h * 4 + 4)
                if first:
                    pe.wait_ge(o_copied, h * O_BLOCKS + n + 1)
                bank, hi, lo = ps_o[n % 2], pt_hi[i % PT_RING], pt_lo[i % PT_RING]
                if kind == "swa":
                    t, at = 2 * step[1], (step[1] % 2) * 2 * P
                    parts = [(t, P, 3 * P, 0, 2 * P), (t - 1, 0, P, 0, P), (t + 1, 3 * P, 4 * P, P, 2 * P)]
                    parts = [x for x in parts if x[0] >= 0]
                    for m, (k, c0, c1, o0, o1) in enumerate(parts):
                        for pt in (hi, lo):
                            last = nc.tensor.matmul(bank[:, at + o0:at + o1], v_st[kind][:, k], pt[:, c0:c1],
                                                    start=(m == 0 and pt is hi),
                                                    stop=(m == len(parts) - 1 and pt is lo),
                                                    skip_group_check=True)
                else:
                    w = turn_width(step)
                    for pt in (hi, lo):
                        last = nc.tensor.matmul(bank[:, BANK - w:BANK], v_st[kind][:, step[2]], pt[:, 0:w],
                                                start=(first and pt is hi), stop=(last_one and pt is lo),
                                                skip_group_check=True)
                last.then_inc(weighted, 1)

            pe.sem_inc(weighted, 1)
            for c in swa_chunks:
                scores(BEFORE, ("next",) + c)
            for g in PRE_TURNS:
                turn_over(BEFORE, g)

            def turn(h, last=False):
                for i in range(NSTEP):
                    for c in chunk_at[i]:
                        if not (last and c[0] == "next"):
                            scores(h, c)
                    for g in turn_at[i]:
                        if not (last and (g[0] == "next" or g[:2] == ("v", "swa"))):
                            turn_over(h, g)
                    weigh(h, i)

            with pe.Fori(0, H - 1) as h:
                turn(h)
            turn(H - 1, True)

        @block.vector
        def _(dve):
            def score(h, c):
                ring = chunk_ring(c)
                kind = c[1] if c[0] == "next" else c[0]
                dve.wait_ge(summed, chunk_count(h, c))
                if kind == "swa":
                    j = c[2]
                    if j == 0:
                        dve.wait_ge(qk_loaded["swa"], 128 * (h + 1) + 128)
                        nc.vector.tensor_scalar(sink_neg[:], sink[:], -1.0, None, ALU.mult).then_inc(sink_negated, 1)
                        dve.wait_ge(sink_negated, h + 2)
                        if h is not BEFORE:
                            dve.wait_ge(turned, turn_count(h, ("p", BLOCK0[3] - 1)))
                            dve.wait_ge(sink_exped, h + 1)
                    nc.vector.nop(nofuse=True)
                    for n in range(2):
                        t = 2 * j + n
                        lo = 0 if t else P
                        last = nc.vector.tensor_tensor_reduce(
                            out=swa_cols(t, lo, 2 * P), in0=ps_s[ring][:, n * 2 * P + lo:(n + 1) * 2 * P],
                            in1=alibi[:, lo:], scale=-SCALE, scalar=sink_neg[:], op0=ALU.add, op1=ALU.min,
                            accum_out=neg_max["swa"][:, t:t + 1])
                else:
                    _, b, t, n = c
                    if (b, t, n) == (0, 0, 0):
                        dve.wait_ge(qk_loaded["fox"], 112 * h + 112)
                        dve.wait_ge(turned, turn_count(h - 1, ("p", NSTEP - 1)))
                    if (b, t, n) == (2, 0, 0):
                        dve.wait_ge(turned, turn_count(h, ("p", QT // 2 - 1)))
                    if (b, t, n) == (3, 0, 0):
                        dve.wait_ge(turned, turn_count(h, ("p", BLOCK0[2] - 1)))
                    w = width(b, t, n)
                    nm = neg_max["fox"][:, 4 * b + t]
                    if n:
                        dve.wait_ge(scored, chunk_count(h, c) - 1)
                    nc.vector.nop(nofuse=True)
                    last = nc.vector.tensor_tensor_reduce(
                        out=p_cols(b, t, n * BANK, n * BANK + w), in0=ps_s[ring][:, 0:w],
                        in1=decay_sb[:, n * BANK:n * BANK + w], scale=-SCALE,
                        scalar=nm[:, n - 1:n] if n else FLT_MAX, op0=ALU.add, op1=ALU.min,
                        accum_out=nm[:, n:n + 1])
                last.then_inc(scored, 1)

            def copy_out(h, g):
                bank = ps_t[order_of(h).index(g) % T_RING]
                what = g[1:] if g[0] == "next" else g
                if what[0] == "p":
                    head, i = (h + 1 if g[0] == "next" else h), what[1]
                    lo, hi = turned_cols(i)
                    dve.wait_ge(p_hi_done, head * NSTEP + i + 1)
                    nc.vector.tensor_tensor(pt_lo[i % PT_RING][:, lo:hi], bank[:, lo:hi],
                                            pt_hi[i % PT_RING][:, lo:hi].bitcast(F32),
                                            ALU.subtract).then_inc(p_lo_done, 1)
                elif what[0] == "v":
                    pass
                else:
                    dve.wait_ge(turned, turn_count(h, g))
                    dve.wait_ge(r_stored, 16 + 32 * h)
                    nc.vector.tensor_copy(recip_t[:], bank[0:2 * QT, 0:P]).then_inc(r_copied, 1)

            def invert_swa(h):
                dve.wait_ge(sink_exped, h + 1)
                dve.wait_ge(r_copied, h + 1)
                nc.vector.tensor_tensor(sink_exp[:], sink_exp[:], rsum["swa"][:], ALU.add).then_inc(denom_done, 1)
                dve.wait_ge(denom_done, h + 1)
                nc.vector.reciprocal(recip[:, 0:QT], sink_exp[:]).then_inc(recip_done, 1)

            def invert_fox(h):
                dve.wait_ge(exped, tile_count(h, ("fox", QB - 1, 3)))
                nc.vector.reciprocal(recip[:, QT:2 * QT], rsum["fox"][:]).then_inc(recip_done, 1)

            for done in (recip_done, r_copied, p_lo_done):
                dve.sem_inc(done, 1)
            dve.wait_ge(const_in, 32)
            nc.vector.tensor_copy(ident_r[:], ident[:]).then_inc(const_r, 1)
            nc.vector.tensor_copy(causal_r[:], causal[:]).then_inc(const_r, 1)
            for c in swa_chunks:
                score(BEFORE, ("next",) + c)
            for g in PRE_TURNS:
                copy_out(BEFORE, g)

            def turn(h, last=False):
                for i in range(NSTEP):
                    for c in chunk_at[i]:
                        if not (last and c[0] == "next"):
                            score(h, c)
                    if i == 4:
                        invert_swa(h)
                    if i == 36:
                        invert_fox(h)
                    for g in turn_at[i]:
                        if not (last and (g[0] == "next" or g[:2] == ("v", "swa"))):
                            copy_out(h, g)

            with dve.Fori(0, H - 1) as h:
                turn(h)
            turn(H - 1, True)

        @block.scalar
        def _(act):
            def exponentiate(h, c):
                if c[0] == "next":
                    if c[2] == 0 and h is not BEFORE:
                        act.wait_ge(recip_done, 2 * h + 2)
                    act.wait_ge(scored, chunk_count(h, c))
                    for t in (2 * c[2], 2 * c[2] + 1):
                        cols = swa_cols(t, 0 if t else P, 2 * P)
                        nc.scalar.activation(cols, cols, ACT.Exp, scale=-1.0, bias=neg_max["swa"][:, t:t + 1],
                                             accum_out=rsum["swa"][:, t:t + 1]).then_inc(exped, 1)
                elif c[3] == c[1]:
                    _, b, t, _ = c
                    if (b, t) == (0, 0):
                        act.wait_ge(recip_done, 2 * h + 1)
                    act.wait_ge(scored, chunk_count(h, c))
                    cols = p_cols(b, t, 0, (4 * b + t + 1) * P)
                    nc.scalar.activation(cols, cols, ACT.Exp, scale=-1.0, bias=neg_max["fox"][:, 4 * b + t, b:b + 1],
                                         accum_out=rsum["fox"][:, 4 * b + t:4 * b + t + 1]).then_inc(exped, 1)

            def copy_hi(h, g):
                what = g[1:] if g[0] == "next" else g
                bank = ps_t[order_of(h).index(g) % T_RING]
                if what[0] == "r":
                    return
                if what[0] == "v":
                    kind, m = what[1:]
                    act.wait_ge(turned, turn_count(h, g))
                    if m == 0 and h is not BEFORE:
                        act.wait_ge(weighted, h * NSTEP + (QT // 2 if kind == "swa" else 0) + 1)
                    nc.scalar.activation(v_st[kind][:, 4 * m:4 * m + 4],
                                         bank[:].rearrange("p (k d) -> p k d", d=P), ACT.Copy).then_inc(v_done[kind], 1)
                    return
                head, i = (h + 1 if g[0] == "next" else h), what[1]
                lo, hi = turned_cols(i)
                act.wait_ge(turned, turn_count(h, g))
                if h is not BEFORE:
                    act.wait_ge(weighted, head * NSTEP + i - PT_RING + 2)
                nc.scalar.activation(pt_hi[i % PT_RING][:, lo:hi], bank[:, lo:hi], ACT.Copy).then_inc(p_hi_done, 1)

            def copy_outputs(h, i):
                n, _, last_one = o_block(steps[i])
                if last_one:
                    act.wait_ge(weighted, h * NSTEP + i + 2)
                    act.wait_ge(o_stored[n % O_RING], 16 + 32 * (h * (O_BLOCKS // O_RING) + n // O_RING))
                    nc.scalar.activation(o_sb[n % O_RING][:], ps_o[n % 2][:], ACT.Copy).then_inc(o_copied, 1)

            def weigh_sinks(h):
                act.wait_ge(scored, chunk_count(h, ("swa", QT // 2 - 1)))
                act.wait_ge(recip_done, 2 * h + 1)
                nc.scalar.activation(sink_exp[:], neg_max["swa"][:], ACT.Exp, bias=sink[:]).then_inc(sink_exped, 1)

            act.sem_inc(o_copied, 2)
            for c in swa_chunks:
                exponentiate(BEFORE, ("next",) + c)
            for g in PRE_TURNS:
                copy_hi(BEFORE, g)

            def turn(h, last=False):
                for i in range(NSTEP):
                    for c in chunk_at[i - 1] if i else []:
                        if not (last and c[0] == "next"):
                            exponentiate(h, c)
                    for g in turn_at[i]:
                        if not (last and (g[0] == "next" or g[:2] == ("v", "swa"))):
                            copy_hi(h, g)
                    if i == 2:
                        weigh_sinks(h)
                    if i:
                        copy_outputs(h, i - 1)
                copy_outputs(h, NSTEP - 1)

            with act.Fori(0, H - 1) as h:
                turn(h)
            turn(H - 1, True)


def tables():
    import numpy as np

    scale = float(HEAD_DIM) ** -0.5
    q, k = np.arange(P)[:, None], np.arange(P)[None, :]
    causal = np.where(k > q, NEG, 0.0).astype(np.float32)
    k = np.arange(2 * P)[None, :] - P
    band = (k // CHUNK <= q // CHUNK) & (k // CHUNK >= q // CHUNK - 1)
    slopes = 2.0 ** (-8.0 * np.arange(1, SWA_HEADS + 1) / SWA_HEADS)
    alibi = np.where(band, -slopes[:, None, None] * np.abs(q - k) / scale, NEG).astype(np.float32)
    return causal, alibi


def mix_out(nc, o_main, o_rest, rsum_inv, w_out, x, norm_mlp, ident_dram, x_mid, h_hi_dram, h_lo_dram):
    E, S = o_main.shape
    D = w_out.shape[1]
    EK, DK, ST = E // P, D // P, S // P
    HALVES = D // BANK
    PAIRS = ST // 2
    with ExitStack() as ctx:
        sb, pb, sem = scopes(nc, ctx)
        ident = sb("m_ident", [P, P])
        gain = sb("m_gain", [P, D])
        mhalf = sb("m_mhalf", [P, 1])
        w_raw = sb("m_w_raw", [P, EK, D])
        w_hi = sb("m_w_hi", [P, EK, D], F32R)
        w_lo = sb("m_w_lo", [P, EK, D], F32R)
        mix = sb("m_mix", [P, 2, EK, P])
        rest = sb("m_rest", [P, 2, EK, P])
        inv = sb("m_inv", [P, 2, EK, P])
        mix_hi = sb("m_mix_hi", [P, 2, EK, P], F32R)
        mix_lo = sb("m_mix_lo", [P, 2, EK, P], F32R)
        x_in = sb("m_x_in", [P, 2, D])
        xm = sb("m_xm", [P, 2, D])
        xn = sb("m_xn", [P, 2, D])
        ssum = sb("m_ssum", [P, 2])
        rstd = sb("m_rstd", [P, 2])
        ht_hi = sb("m_ht_hi", [P, 2, DK, P])
        ht_hi_r = ht_hi[:].bitcast(F32R)
        ht_lo = sb("m_ht_lo", [P, 2, DK, P])
        ht_lo_r = ht_lo[:].bitcast(F32R)
        ps_o = [pb(f"m_ps_o{i}") for i in range(4)]
        ps_t = [pb(f"m_ps_t{i}") for i in range(4)]

        const_in = sem("m_const_in")
        w_loaded = [sem(f"m_w_loaded{k}") for k in range(EK)]
        w_hi_done = sem("m_w_hi_done")
        w_lo_done = sem("m_w_lo_done")
        o_loaded = [sem(f"m_o_loaded{i}") for i in range(2)]
        x_loaded = [sem(f"m_x_loaded{i}") for i in range(2)]
        mhalf_set = sem("m_mhalf_set")
        joined = sem("m_joined")
        divided = sem("m_divided")
        mix_hi_done = sem("m_mix_hi_done")
        mix_lo_done = sem("m_mix_lo_done")
        summed = sem("m_summed")
        added = sem("m_added")
        x_stored = [sem(f"m_x_stored{i}") for i in range(2)]
        squared = sem("m_squared")
        meaned = sem("m_meaned")
        rooted = sem("m_rooted")
        normed = sem("m_normed")
        turned = sem("m_turned")
        ht_hi_done = sem("m_ht_hi_done")
        ht_lo_done = sem("m_ht_lo_done")
        ht_stored = [sem(f"m_ht_stored{i}") for i in range(2)]

        block = ctx.enter_context(nc.Block())

        def walk(eng, tile):
            tile(0, 0)
            tile(0, 1)
            with eng.Fori(1, PAIRS - 1) as i:
                tile(i, 0)
                tile(i, 1)
            tile(PAIRS - 1, 0)
            tile(PAIRS - 1, 1)

        def is_first(pair, slot):
            return isinstance(pair, int) and (pair, slot) == (0, 0)

        def is_last(pair, slot):
            return isinstance(pair, int) and (pair, slot) == (PAIRS - 1, 1)

        def in_first_pair(pair):
            return isinstance(pair, int) and pair == 0

        @block.sync
        def _(sp):
            def load_mix(pair, slot):
                t = 2 * pair + slot
                s = bass.ds(t * P, P)
                if not in_first_pair(pair):
                    sp.wait_ge(mix_lo_done, t - 1)
                    sp.nop(nofuse=True)
                done = o_loaded[slot]
                sp.dma_start(mix[:, slot], o_main[:, s].rearrange("(k p) s -> p k s", p=P)).then_inc(done, 16)
                sp.dma_start(rest[:, slot], o_rest[:, s].rearrange("(k p) s -> p k s", p=P)).then_inc(done, 16)
                for half in range(2):
                    rows = slice(half * HEAD_DIM, (half + 1) * HEAD_DIM)
                    src = rsum_inv[:, s].rearrange("(k two) s -> two k s", two=2)[half]
                    sp.dma_start(inv[rows, slot], src.partition_broadcast(HEAD_DIM)).then_inc(done, 16)

            def load_x(pair, slot):
                t = 2 * pair + slot
                if not in_first_pair(pair):
                    sp.wait_ge(added, 2 * (t - 1))
                    sp.nop(nofuse=True)
                sp.dma_start(x_in[:, slot], x[bass.ds(t * P, P), :]).then_inc(x_loaded[slot], 16)

            def store_ht(pair, slot):
                t = 2 * pair + slot
                sp.wait_ge(ht_lo_done, 2 * t + 2)
                sp.nop(nofuse=True)
                for part, dst in ((ht_hi, h_hi_dram), (ht_lo, h_lo_dram)):
                    sp.dma_start(dst[:, bass.ds(t * P, P)].rearrange("(k p) s -> p k s", p=P),
                                 part[:, slot]).then_inc(ht_stored[slot], 16)

            for done in ht_stored:
                sp.sem_inc(done, 16)
            load_mix(0, 0)
            for k in range(EK):
                sp.dma_start(w_raw[:, k], w_out[k * P:(k + 1) * P, :]).then_inc(w_loaded[k], 16)
            sp.dma_start(ident[:], ident_dram).then_inc(const_in, 16)
            sp.dma_start(gain[:], norm_mlp[0].partition_broadcast(P)).then_inc(const_in, 16)
            load_mix(0, 1)
            load_x(0, 0)
            load_x(0, 1)

            def tile(pair, slot):
                t = 2 * pair + slot
                ends = isinstance(pair, int) and pair == PAIRS - 1
                if not ends:
                    load_mix(pair + 1, slot)
                sp.wait_ge(added, 2 * t + 2)
                sp.nop(nofuse=True)
                sp.dma_start(x_mid[bass.ds(t * P, P), :], xm[:, slot]).then_inc(x_stored[slot], 16)
                if not ends:
                    load_x(pair + 1, slot)
                if not is_first(pair, slot):
                    store_ht(pair - 1 + slot, 1 - slot)

            walk(sp, tile)
            store_ht(PAIRS - 1, 1)
            for slot in range(2):
                sp.wait_ge(x_stored[slot], 16 * PAIRS)
                sp.wait_ge(ht_stored[slot], 16 + 32 * PAIRS)

        @block.gpsimd
        def _(pool):
            def join(pair, slot):
                pool.wait_ge(o_loaded[slot], 64 * (pair + 1))
                nc.gpsimd.tensor_tensor(mix[:, slot], mix[:, slot], rest[:, slot], ALU.add).then_inc(joined, 1)

            join(0, 0)
            pool.wait_ge(mhalf_set, 1)

            def tile(pair, slot):
                t = 2 * pair + slot
                if not is_last(pair, slot):
                    join(pair + slot, 1 - slot)
                pool.wait_ge(squared, t + 1)
                nc.gpsimd.nop(nofuse=True)
                nc.gpsimd.tensor_scalar(rstd[:, slot:slot + 1], ssum[:, slot:slot + 1], 1.0 / D, EPS,
                                        ALU.mult, ALU.add).then_inc(meaned, 1)
                pool.wait_ge(meaned, t + 1)
                nc.gpsimd.tensor_tensor(rstd[:, slot:slot + 1], rstd[:, slot:slot + 1], mhalf[:],
                                        ALU.pow).then_inc(rooted, 1)

            walk(pool, tile)

        @block.scalar
        def _(act):
            def split_mix(pair, slot):
                t = 2 * pair + slot
                act.wait_ge(divided, t + 1)
                if not in_first_pair(pair):
                    act.wait_ge(summed, HALVES * (t - 1))
                nc.scalar.activation(mix_hi[:, slot], mix[:, slot], ACT.Copy).then_inc(mix_hi_done, 1)

            def split_ht(pair, slot):
                t = 2 * pair + slot
                act.wait_ge(ht_stored[slot], 16 + 32 * pair)
                for half in range(2):
                    act.wait_ge(turned, 2 * t + half + 1)
                    nc.scalar.activation(ht_hi_r[:, slot, 4 * half:4 * half + 4],
                                         ps_t[2 * slot + half][:].rearrange("p (k s) -> p k s", s=P),
                                         ACT.Copy).then_inc(ht_hi_done, 1)

            split_mix(0, 0)
            for k in range(EK):
                act.wait_ge(w_loaded[k], 16)
                nc.scalar.activation(w_hi[:, k], w_raw[:, k], ACT.Copy).then_inc(w_hi_done, 1)

            def tile(pair, slot):
                t = 2 * pair + slot
                if not is_last(pair, slot):
                    split_mix(pair + slot, 1 - slot)
                act.wait_ge(added, 2 * t + 2)
                if not in_first_pair(pair):
                    act.wait_ge(turned, 2 * (t - 1))
                nc.scalar.activation(xn[:, slot], xm[:, slot], ACT.Square,
                                     accum_out=ssum[:, slot:slot + 1]).then_inc(squared, 1)
                if not is_first(pair, slot):
                    split_ht(pair - 1 + slot, 1 - slot)

            walk(act, tile)
            split_ht(PAIRS - 1, 1)

        @block.vector
        def _(dve):
            def divide(pair, slot):
                dve.wait_ge(joined, 2 * pair + slot + 1)
                nc.vector.tensor_tensor(mix[:, slot], mix[:, slot], inv[:, slot], ALU.mult).then_inc(divided, 1)

            def split_mix(pair, slot):
                dve.wait_ge(mix_hi_done, 2 * pair + slot + 1)
                nc.vector.tensor_tensor(mix_lo[:, slot], mix[:, slot], mix_hi[:, slot].bitcast(F32),
                                        ALU.subtract).then_inc(mix_lo_done, 1)

            def split_ht(pair, slot):
                t = 2 * pair + slot
                for half in range(2):
                    k = slice(4 * half, 4 * half + 4)
                    dve.wait_ge(ht_hi_done, 2 * t + half + 1)
                    nc.vector.tensor_tensor(ht_lo_r[:, slot, k],
                                            ps_t[2 * slot + half][:].rearrange("p (k s) -> p k s", s=P),
                                            ht_hi[:, slot, k], ALU.subtract).then_inc(ht_lo_done, 1)

            nc.vector.memset(mhalf[:], -0.5).then_inc(mhalf_set, 1)
            divide(0, 0)
            split_mix(0, 0)
            for k in range(EK):
                dve.wait_ge(w_hi_done, k + 1)
                nc.vector.tensor_tensor(w_lo[:, k], w_raw[:, k], w_hi[:, k].bitcast(F32),
                                        ALU.subtract).then_inc(w_lo_done, 1)

            def tile(pair, slot):
                t = 2 * pair + slot
                if not is_last(pair, slot):
                    divide(pair + slot, 1 - slot)
                    split_mix(pair + slot, 1 - slot)
                dve.wait_ge(x_loaded[slot], 16 * (pair + 1))
                dve.wait_ge(x_stored[slot], 16 * pair)
                for half in range(HALVES):
                    cols = slice(half * BANK, (half + 1) * BANK)
                    dve.wait_ge(summed, HALVES * t + half + 1)
                    nc.vector.tensor_tensor(xm[:, slot, cols], ps_o[2 * slot + half][:], x_in[:, slot, cols],
                                            ALU.add).then_inc(added, 1)
                if not is_first(pair, slot):
                    split_ht(pair - 1 + slot, 1 - slot)
                else:
                    dve.wait_ge(const_in, 32)
                dve.wait_ge(rooted, t + 1)
                nc.vector.scalar_tensor_tensor(xn[:, slot], xm[:, slot], rstd[:, slot:slot + 1], gain[:],
                                               ALU.mult, ALU.mult).then_inc(normed, 1)

            walk(dve, tile)
            split_ht(PAIRS - 1, 1)

        @block.tensor
        def _(pe):
            def turn(pair, slot):
                t = 2 * pair + slot
                pe.wait_ge(normed, t + 1)
                if not in_first_pair(pair):
                    pe.wait_ge(ht_lo_done, 2 * (t - 1))
                for half in range(2):
                    for k in range(4):
                        col = (4 * half + k) * P
                        last = nc.tensor.transpose(ps_t[2 * slot + half][:, k * P:(k + 1) * P],
                                                   xn[:, slot, col:col + P], ident[:])
                    last.then_inc(turned, 1)

            def tile(pair, slot):
                t = 2 * pair + slot
                pe.wait_ge(mix_lo_done, t + 1)
                for half in range(HALVES):
                    if not in_first_pair(pair):
                        pe.wait_ge(added, HALVES * t - 3 + half)
                    cols = slice(half * BANK, (half + 1) * BANK)
                    for k in range(EK):
                        if is_first(pair, slot) and half == 0:
                            pe.wait_ge(w_lo_done, k + 1)
                        for n, (m, w) in enumerate(((mix_hi, w_hi), (mix_hi, w_lo), (mix_lo, w_hi))):
                            last = nc.tensor.matmul(ps_o[2 * slot + half][:], m[:, slot, k], w[:, k, cols],
                                                    start=(k == 0 and n == 0), stop=(k == EK - 1 and n == 2))
                    last.then_inc(summed, 1)
                if is_first(pair, slot):
                    pe.wait_ge(const_in, 32)
                else:
                    turn(pair - 1 + slot, 1 - slot)

            walk(pe, tile)
            turn(PAIRS - 1, 1)


def mlp(nc, x_mid, h_hi_dram, h_lo_dram, w_up, w_down, norm_final, out):
    S, D = x_mid.shape
    F = w_up.shape[1]
    DK = D // P
    T = 1024
    C = 256
    NB, NC = S // T, F // C
    FT, SBK, ST, HALVES = C // P, T // BANK, T // P, D // BANK
    UPS = FT * SBK
    DOWNS = ST * HALVES
    RING = 4
    with ExitStack() as ctx:
        sb, pb, sem = scopes(nc, ctx)
        gain = sb("f_gain", [P, D])
        mhalf = sb("f_mhalf", [P, 1])
        h_hi = sb("f_h_hi", [P, DK, T], F32R)
        h_lo = sb("f_h_lo", [P, DK, T], F32R)
        acc = sb("f_acc", [P, ST, D])
        u_hi = [sb(f"f_u_hi{i}", [P, FT, T], F32R) for i in range(2)]
        u_lo = [sb(f"f_u_lo{i}", [P, FT, T], F32R) for i in range(2)]
        wu_raw = sb("f_wu_raw", [P, DK, C])
        wu_hi = sb("f_wu_hi", [P, DK, C], F32R)
        wu_lo = sb("f_wu_lo", [P, DK, C], F32R)
        wd_raw = sb("f_wd_raw", [P, FT, D])
        wd_hi = sb("f_wd_hi", [P, FT, D], F32R)
        wd_lo = sb("f_wd_lo", [P, FT, D], F32R)
        r = sb("f_r", [P, 2, BANK])
        sq = sb("f_sq", [P, 2, BANK])
        y = sb("f_y", [P, 2, D])
        ssum = sb("f_ssum", [P, 2])
        rstd = sb("f_rstd", [P, 2])
        ps_u = [pb(f"f_ps_u{i}") for i in range(RING)]
        ps_d = [pb(f"f_ps_d{i}") for i in range(RING)]

        const_in = sem("f_const_in")
        mhalf_set = sem("f_mhalf_set")
        h_loaded = [sem(f"f_h_loaded{i}") for i in range(SBK)]
        acc_loaded = sem("f_acc_loaded")
        wu_loaded = sem("f_wu_loaded")
        wu_hi_done = sem("f_wu_hi_done")
        wu_lo_done = sem("f_wu_lo_done")
        wd_loaded = sem("f_wd_loaded")
        wd_hi_done = sem("f_wd_hi_done")
        wd_lo_done = sem("f_wd_lo_done")
        upped = sem("f_upped")
        relu_done = sem("f_relu_done")
        sq_done = sem("f_sq_done")
        u_hi_done = sem("f_u_hi_done")
        u_lo_done = sem("f_u_lo_done")
        downed = sem("f_downed")
        added = sem("f_added")
        squared = sem("f_squared")
        meaned = sem("f_meaned")
        rooted = sem("f_rooted")
        normed = sem("f_normed")
        stored = [sem(f"f_stored{i}") for i in range(2)]

        wu_v = w_up.rearrange("(k p) f -> p k f", p=P)
        wd_v = w_down.rearrange("(c k p) d -> c p k d", p=P, k=FT)
        block = ctx.enter_context(nc.Block())

        def walk(eng, step):
            def block_of(b):
                step(b, 0, 0)
                with eng.Fori(0, (NC - 4) // 2) as j:
                    step(b, 2 * j + 1, 1)
                    step(b, 2 * j + 2, 0)
                for c in range(NC - 3, NC):
                    step(b, c, c % 2)
            return block_of

        @block.sync
        def _(sp):
            def load_up(b, c):
                g = b * NC + c
                if not (isinstance(g, int) and g == 0):
                    sp.wait_ge(wu_lo_done, g)
                sp.dma_start(wu_raw[:], wu_v[:, :, bass.ds(c * C, C)]).then_inc(wu_loaded, 16)

            def load_down(b, c):
                g = b * NC + c
                if not (isinstance(g, int) and g == 0):
                    sp.wait_ge(wd_lo_done, g)
                sp.dma_start(wd_raw[:], wd_v[bass.ds(c, 1)].rearrange("a p k d -> (a p) k d")).then_inc(wd_loaded, 16)

            def load_h(b):
                for s in range(SBK):
                    cols = slice(b * T + s * BANK, b * T + (s + 1) * BANK)
                    for dst, src in ((h_hi, h_hi_dram), (h_lo, h_lo_dram)):
                        sp.dma_start(dst[:, :, s * BANK:(s + 1) * BANK].bitcast(F32),
                                     src[:, cols].rearrange("(k p) s -> p k s", p=P)).then_inc(h_loaded[s], 16)

            def load_acc(b, t):
                row = b * T + t * P
                if b:
                    sp.wait_ge(normed, (b - 1) * ST + t + 1)
                sp.dma_start(acc[:, t], x_mid[row:row + P, :]).then_inc(acc_loaded, 16)

            def store(b, t):
                row = b * T + t * P
                sp.wait_ge(normed, b * ST + t + 1)
                sp.dma_start(out[row:row + P, :], y[:, t % 2]).then_inc(stored[t % 2], 16)

            def step(b, c, parity):
                last = isinstance(c, int) and c == NC - 1
                if not last:
                    load_down(b, c + 1)
                    if isinstance(c, int) and c == NC - 2:
                        if b + 1 < NB:
                            load_up(b + 1, 0)
                    else:
                        load_up(b, c + 2)
                elif b + 1 < NB:
                    sp.wait_ge(upped, (b + 1) * NC * UPS)
                    load_h(b + 1)
                    load_up(b + 1, 1)
                    load_down(b + 1, 0)
                    for t in range(ST):
                        store(b, t)
                        load_acc(b + 1, t)
                else:
                    for t in range(ST):
                        store(b, t)

            load_up(0, 0)
            load_h(0)
            load_down(0, 0)
            sp.dma_start(gain[:], norm_final.partition_broadcast(P)).then_inc(const_in, 16)
            load_up(0, 1)
            for t in range(ST):
                load_acc(0, t)
            for b in range(NB):
                walk(sp, step)(b)
            for i in range(2):
                sp.wait_ge(stored[i], 16 * NB * ST // 2)

        @block.gpsimd
        def _(pool):
            pool.wait_ge(mhalf_set, 1)
            with pool.Fori(0, NB * ST // 2) as i:
                for slot in range(2):
                    pool.wait_ge(squared, 2 * i + slot + 1)
                    nc.gpsimd.nop(nofuse=True)
                    nc.gpsimd.tensor_scalar(rstd[:, slot:slot + 1], ssum[:, slot:slot + 1], 1.0 / D, EPS,
                                            ALU.mult, ALU.add).then_inc(meaned, 1)
                    pool.wait_ge(meaned, 2 * i + slot + 1)
                    nc.gpsimd.tensor_tensor(rstd[:, slot:slot + 1], rstd[:, slot:slot + 1], mhalf[:],
                                            ALU.pow).then_inc(rooted, 1)

        @block.scalar
        def _(act):
            def split_up(g):
                act.wait_ge(wu_loaded, 16 * (g + 1))
                if not (isinstance(g, int) and g == 0):
                    act.wait_ge(upped, g * UPS)
                nc.scalar.activation(wu_hi[:], wu_raw[:], ACT.Copy).then_inc(wu_hi_done, 1)

            def split_down(g):
                act.wait_ge(wd_loaded, 16 * (g + 1))
                if not (isinstance(g, int) and g == 0):
                    act.wait_ge(downed, g * DOWNS)
                nc.scalar.activation(wd_hi[:], wd_raw[:], ACT.Copy).then_inc(wd_hi_done, 1)

            def activate(g, parity, n):
                q = g * UPS + n
                act.wait_ge(upped, q + 1)
                if not (isinstance(g, int) and q < 2):
                    act.wait_ge(sq_done, q - 1)
                nc.scalar.activation(r[:, n % 2], ps_u[n][:], ACT.Relu).then_inc(relu_done, 1)
                act.wait_ge(sq_done, q + 1)
                f, s = divmod(n, SBK)
                nc.scalar.activation(u_hi[parity][:, f, s * BANK:(s + 1) * BANK], sq[:, n % 2],
                                     ACT.Copy).then_inc(u_hi_done, 1)

            def square_sums(b):
                for t in range(ST):
                    act.wait_ge(added, (b * NC + NC - 1) * DOWNS + HALVES * (t + 1))
                    if t >= 2 or b:
                        act.wait_ge(stored[t % 2], 16 * ((b * ST + t) // 2))
                    nc.scalar.activation(y[:, t % 2], acc[:, t], ACT.Square,
                                         accum_out=ssum[:, t % 2:t % 2 + 1]).then_inc(squared, 1)

            def step(b, c, parity):
                g = b * NC + c
                if isinstance(c, int) and c == NC - 1:
                    split_down(g)
                    square_sums(b)
                    return
                if isinstance(c, int) and c == 0:
                    if b == 0:
                        split_up(0)
                    for n in range(UPS):
                        activate(g, 0, n)
                    split_up(g + 1)
                activate(g + 1, 1 - parity, 0)
                split_down(g)
                for n in range(1, UPS):
                    activate(g + 1, 1 - parity, n)
                if not (isinstance(c, int) and c == NC - 2) or b + 1 < NB:
                    split_up(g + 2)

            for b in range(NB):
                walk(act, step)(b)

        @block.vector
        def _(dve):
            def split_up(g):
                dve.wait_ge(wu_hi_done, g + 1)
                nc.vector.tensor_tensor(wu_lo[:], wu_raw[:], wu_hi[:].bitcast(F32),
                                        ALU.subtract).then_inc(wu_lo_done, 1)

            def split_down(g):
                dve.wait_ge(wd_hi_done, g + 1)
                nc.vector.tensor_tensor(wd_lo[:], wd_raw[:], wd_hi[:].bitcast(F32),
                                        ALU.subtract).then_inc(wd_lo_done, 1)

            def activate(g, parity, n):
                q = g * UPS + n
                f, s = divmod(n, SBK)
                cols = slice(s * BANK, (s + 1) * BANK)
                dve.wait_ge(relu_done, q + 1)
                nc.vector.tensor_tensor(sq[:, n % 2], r[:, n % 2], r[:, n % 2], ALU.mult).then_inc(sq_done, 1)
                dve.wait_ge(u_hi_done, q + 1)
                nc.vector.tensor_tensor(u_lo[parity][:, f, cols], sq[:, n % 2],
                                        u_hi[parity][:, f, cols].bitcast(F32), ALU.subtract).then_inc(u_lo_done, 1)

            def add(g, n):
                t, half = divmod(n, HALVES)
                cols = slice(half * BANK, (half + 1) * BANK)
                dve.wait_ge(downed, g * DOWNS + n + 1)
                nc.vector.tensor_tensor(acc[:, t, cols], acc[:, t, cols], ps_d[n % RING][:],
                                        ALU.add).then_inc(added, 1)

            def norm(b, t):
                dve.wait_ge(rooted, b * ST + t + 1)
                nc.vector.scalar_tensor_tensor(y[:, t % 2], acc[:, t], rstd[:, t % 2:t % 2 + 1], gain[:],
                                               ALU.mult, ALU.mult).then_inc(normed, 1)

            nc.vector.memset(mhalf[:], -0.5).then_inc(mhalf_set, 1)
            dve.wait_ge(const_in, 16)

            def step(b, c, parity):
                g = b * NC + c
                if isinstance(c, int) and c == NC - 1:
                    split_down(g)
                    for n in range(DOWNS):
                        add(g, n)
                        if n >= 2 * HALVES - 1 and n % HALVES == HALVES - 1:
                            norm(b, n // HALVES - 1)
                    norm(b, ST - 1)
                    return
                if isinstance(c, int) and c == 0:
                    if b == 0:
                        split_up(0)
                    for n in range(UPS):
                        activate(g, 0, n)
                    split_up(g + 1)
                activate(g + 1, 1 - parity, 0)
                split_down(g)
                for n in range(1, UPS):
                    activate(g + 1, 1 - parity, n)
                if isinstance(c, int) and c == 0:
                    dve.wait_ge(acc_loaded, 16 * ST * (b + 1))
                for n in range(DOWNS):
                    if n == 4 and (not (isinstance(c, int) and c == NC - 2) or b + 1 < NB):
                        split_up(g + 2)
                    add(g, n)

            for b in range(NB):
                walk(dve, step)(b)

        @block.tensor
        def _(pe):
            def up(g, parity, b=None):
                pe.wait_ge(wu_lo_done, g + 1)
                for n in range(UPS):
                    f, s = divmod(n, SBK)
                    if b is not None and f == 0:
                        pe.wait_ge(h_loaded[s], 32 * (b + 1))
                    if not (isinstance(g, int) and g == 0):
                        pe.wait_ge(relu_done, (g - 1) * UPS + n + 1)
                    for k in range(DK):
                        for m, (w, h) in enumerate(((wu_hi, h_hi), (wu_hi, h_lo), (wu_lo, h_hi))):
                            last = nc.tensor.matmul(ps_u[n][:], w[:, k, f * P:(f + 1) * P],
                                                    h[:, k, s * BANK:(s + 1) * BANK],
                                                    start=(k == 0 and m == 0), stop=(k == DK - 1 and m == 2))
                    last.then_inc(upped, 1)

            def down(g, parity):
                pe.wait_ge(wd_lo_done, g + 1)
                pe.wait_ge(u_lo_done, (g + 1) * UPS)
                for n in range(DOWNS):
                    t, half = divmod(n, HALVES)
                    q = g * DOWNS + n
                    if not (isinstance(g, int) and q < RING):
                        pe.wait_ge(added, q - RING + 1)
                    for f in range(FT):
                        for m, (u, w) in enumerate(((u_hi, wd_hi), (u_hi, wd_lo), (u_lo, wd_hi))):
                            last = nc.tensor.matmul(ps_d[n % RING][:], u[parity][:, f, t * P:(t + 1) * P],
                                                    w[:, f, half * BANK:(half + 1) * BANK],
                                                    start=(f == 0 and m == 0), stop=(f == FT - 1 and m == 2))
                    last.then_inc(downed, 1)

            def step(b, c, parity):
                g = b * NC + c
                if isinstance(c, int) and c == 0:
                    up(g, 0, b)
                if not (isinstance(c, int) and c == NC - 1):
                    up(g + 1, 1 - parity)
                down(g, parity)

            for b in range(NB):
                walk(pe, step)(b)


def hybrid_block(nc, x, norm_mix, w_in, b_forget, sinks, w_out, norm_mlp, w_up, w_down, norm_final,
                 ident, causal, alibi, out):
    x, out = (a.rearrange("b s d -> (b s) d") for a in (x, out))
    w_in, w_out, w_up, w_down = (w.rearrange("l a b -> (l a) b") for w in (w_in, w_out, w_up, w_down))
    S, D = x.shape
    E = w_out.shape[0]
    rows = -(-w_in.shape[1] // P) * P

    def scratch(name, *shape):
        return nc.dram_tensor(name, shape, F32).ap()

    proj_hi, proj_lo = scratch("proj_hi", rows, S), scratch("proj_lo", rows, S)
    decay = scratch("decay", FOX_HEADS, S)
    o_main, o_rest = scratch("o_main", E, S), scratch("o_rest", E, S)
    rsum_inv = scratch("rsum_inv", SWA_HEADS + FOX_HEADS, S)
    x_mid = scratch("x_mid", S, D)
    h_hi, h_lo = scratch("h_hi", D, S), scratch("h_lo", D, S)

    project(nc, x, norm_mix, w_in, ident, proj_hi, proj_lo)
    gate(nc, proj_hi, proj_lo, b_forget, decay)
    attend(nc, proj_hi, proj_lo, sinks, ident, causal, alibi, decay, o_main, o_rest, rsum_inv)
    mix_out(nc, o_main, o_rest, rsum_inv, w_out, x, norm_mlp, ident, x_mid, h_hi, h_lo)
    mlp(nc, x_mid, h_hi, h_lo, w_up, w_down, norm_final, out)


_INS = ["x", "norm_mix", "w_in", "b_forget", "sinks", "w_out", "norm_mlp", "w_up", "w_down", "norm_final"]


def kernel(**inputs):
    import numpy as np
    import concourse.bacc as bacc
    from concourse.bass_utils import run_bass_kernel_spmd

    nc = bacc.Bacc("TRN2", target_bir_lowering=False, num_devices=1)
    arrays = {name: np.ascontiguousarray(inputs[name]) for name in _INS}
    causal, alibi = tables()
    arrays |= {"ident": np.eye(P, dtype=np.float32), "causal": causal, "alibi": alibi}
    args = [nc.dram_tensor(f"in_{name}", a.shape, mybir.dt.from_np(a.dtype), kind="ExternalInput").ap()
            for name, a in arrays.items()]
    shape = arrays["x"].shape
    out = nc.dram_tensor("out_0", shape, F32, kind="ExternalOutput").ap()
    hybrid_block(nc, *args, out)
    r = run_bass_kernel_spmd(nc, [{f"in_{name}": a for name, a in arrays.items()}], core_ids=[0])
    return r.results[0]["out_0"]
```

```python
from contextlib import ExitStack

import concourse.bass as bass
from concourse import mybir

F32 = mybir.dt.float32
F32R = mybir.dt.float32r
ALU = mybir.AluOpType
ACT = mybir.ActivationFunctionType

P = 128
EPS = 1e-6
CHUNK = 64
HEAD_DIM = 64
SWA_HEADS = 8
SWA_KV_HEADS = 2
FOX_HEADS = 8
NEG = -1e30
BANK = 512


def scopes(nc, ctx):
    def sb(name, shape, dt=F32):
        return ctx.enter_context(nc.sbuf_tensor(name, shape, dt))

    def pb(name, n=BANK, rows=P):
        return ctx.enter_context(nc.psum_tensor(name, [rows, n], F32))

    def sem(name):
        return ctx.enter_context(nc.semaphore(name))

    return sb, pb, sem


def project(nc, x, norm_mix, w_in, b_forget, ident_dram, proj_hi, proj_lo, decay):
    S, D = x.shape
    DK = D // P
    ST = S // P
    SB = S // BANK
    TPB = ST // SB
    N_IN = w_in.shape[1]
    NCH = -(-N_IN // P)
    LAST = N_IN - P
    X_RING = 4
    GATES = slice(P - 32, P)
    with ExitStack() as ctx:
        sb, pb, sem = scopes(nc, ctx)
        ident = sb("p_ident", [P, P])
        gain = sb("p_gain", [P, D])
        mhalf = sb("p_mhalf", [P, 1])
        bias = sb("p_bias", [P, 1])
        ones = sb("p_ones", [P, 1])
        x_in = sb("p_x_in", [P, X_RING, D])
        ssum = sb("p_ssum", [P, ST])
        rstd = sb("p_rstd", [P, ST])
        ht_hi = sb("p_ht_hi", [P, DK, S], F32R)
        ht_lo = sb("p_ht_lo", [P, DK, S], F32R)
        w_raw = sb("p_w_raw", [P, 2, DK, P])
        w_hi = sb("p_w_hi", [P, 2, DK, P], F32R)
        w_lo = sb("p_w_lo", [P, 2, DK, P], F32R)
        o_hi = sb("p_o_hi", [P, 2, S], F32R)
        o_lo = sb("p_o_lo", [P, 2, S], F32R)
        ps_t = [pb(f"p_ps_t{i}") for i in range(4)]
        ps_o = [pb(f"p_ps_o{i}") for i in range(4)]

        const_in = sem("p_const_in")
        x_loaded = [sem(f"p_x_loaded{i}") for i in range(X_RING)]
        w_loaded = [sem(f"p_w_loaded{i}") for i in range(2)]
        mhalf_set = sem("p_mhalf_set")
        squared = sem("p_squared")
        meaned = sem("p_meaned")
        rooted = sem("p_rooted")
        normed = sem("p_normed")
        turned = sem("p_turned")
        ht_hi_done = sem("p_ht_hi_done")
        ht_lo_done = sem("p_ht_lo_done")
        w_hi_done = sem("p_w_hi_done")
        w_lo_done = sem("p_w_lo_done")
        summed = sem("p_summed")
        o_hi_done = sem("p_o_hi_done")
        o_lo_done = sem("p_o_lo_done")
        stored = [sem(f"p_stored{i}") for i in range(2)]
        bias_set = sem("p_bias_set")
        bias_in = sem("p_bias_in")
        gate_step = sem("p_gate_step")
        log_step = sem("p_log_step")
        decay_stored = sem("p_decay_stored")

        gates = x_in[GATES, 0:2].rearrange("p a d -> p (a d)")
        logs = x_in[GATES, 2:4].rearrange("p a d -> p (a d)")
        squares = o_hi[:, :, S - BANK:S].bitcast(F32)
        assert 2 * D == S and D == 2 * BANK

        x_tiles = x.rearrange("(t p) d -> t p d", p=P)
        w_v = w_in.rearrange("(k p) n -> p k n", p=P)
        block = ctx.enter_context(nc.Block())

        PAIRS = NCH // 2
        assert NCH == 2 * PAIRS + 1 and LAST > (NCH - 2) * P

        product_after_turn = {t: 2 * (t // TPB - 1) + t % TPB // 2 for t in range(TPB, ST) if t % 2}
        product_before_turn = {t + 1: n for t, n in product_after_turn.items() if t + 1 < ST}

        @block.sync
        def _(sp):
            def load_weights(pair, slot, col):
                if not isinstance(pair, int) or pair >= 1:
                    sp.wait_ge(w_lo_done, 2 * pair + slot - 1)
                sp.dma_start(w_raw[:, slot], w_v[:, :, bass.ds(col, P)]).then_inc(w_loaded[slot], 16)

            def store(pair, slot):
                n = 2 * pair + slot
                sp.wait_ge(o_lo_done, 2 * SB if isinstance(pair, int) and pair == 0 else (n + 1) * SB)
                sp.dma_start(proj_hi[bass.ds(n * P, P), :], o_hi[:, slot].bitcast(F32)).then_inc(stored[slot], 16)
                sp.dma_start(proj_lo[bass.ds(n * P, P), :], o_lo[:, slot].bitcast(F32)).then_inc(stored[slot], 16)

            sp.dma_start(x_in[:, 0], x_tiles[0]).then_inc(x_loaded[0], 16)
            sp.dma_start(gain[:], norm_mix[0].partition_broadcast(P)).then_inc(const_in, 16)
            sp.dma_start(ident[:], ident_dram).then_inc(const_in, 16)
            for t in range(1, X_RING):
                sp.dma_start(x_in[:, t], x_tiles[t]).then_inc(x_loaded[t], 16)
            load_weights(0, 0, LAST)
            load_weights(0, 1, 0)
            sp.wait_ge(bias_set, 1)
            sp.dma_start(bias[P - FOX_HEADS:P], b_forget.rearrange("a g -> g a")).then_inc(bias_in, 16)
            for t in range(X_RING, ST):
                sp.wait_ge(turned, 2 * (t - X_RING + 1))
                sp.dma_start(x_in[:, t % X_RING], x_tiles[t]).then_inc(x_loaded[t % X_RING], 16)
            for slot in range(2):
                load_weights(1, slot, (1 + slot) * P)
            for slot in range(2):
                store(0, slot)
            with sp.Fori(1, PAIRS - 1) as i:
                for slot in range(2):
                    load_weights(i + 1, slot, (2 * i + 1 + slot) * P)
                    store(i, slot)
            load_weights(PAIRS, 0, (2 * PAIRS - 1) * P)
            store(PAIRS - 1, 0)
            store(PAIRS - 1, 1)
            sp.wait_ge(gate_step, 6)
            sp.dma_start(decay, logs[32 - FOX_HEADS:32]).then_inc(decay_stored, 16)
            for b in range(SB):
                n, cols = NCH - 1, slice(b * BANK, (b + 1) * BANK)
                sp.wait_ge(o_lo_done, n * SB + b + 1)
                for part, dst in ((o_hi, proj_hi), (o_lo, proj_lo)):
                    sp.dma_start(dst[n * P:(n + 1) * P, cols], part[:, 0, cols].bitcast(F32)).then_inc(stored[0], 16)
            sp.wait_ge(stored[0], 32 * (PAIRS + SB))
            sp.wait_ge(stored[1], 32 * PAIRS)
            sp.wait_ge(decay_stored, 16)

        @block.gpsimd
        def _(pool):
            for t in range(ST):
                pool.wait_ge(squared, t + 1)
                nc.gpsimd.tensor_scalar(rstd[:, t:t + 1], ssum[:, t:t + 1], 1.0 / D, EPS,
                                        ALU.mult, ALU.add).then_inc(meaned, 1)
                pool.wait_ge(meaned, t + 1)
                if t == 0:
                    pool.wait_ge(mhalf_set, 1)
                nc.gpsimd.tensor_tensor(rstd[:, t:t + 1], rstd[:, t:t + 1], mhalf[:],
                                        ALU.pow).then_inc(rooted, 1)

        @block.scalar
        def _(act):
            def square(t):
                act.wait_ge(x_loaded[t % X_RING], 16 * (t // X_RING + 1))
                if t:
                    act.wait_ge(squared, t)
                nc.scalar.activation(squares, x_in[:, t % X_RING].rearrange("p (a d) -> p a d", d=BANK), ACT.Square,
                                     accum_out=ssum[:, t:t + 1]).then_inc(squared, 1)

            def split_ht_hi(t):
                for half in range(2):
                    act.wait_ge(turned, 2 * t + half + 1)
                    nc.scalar.activation(
                        ht_hi[:, 4 * half:4 * half + 4, t * P:(t + 1) * P],
                        ps_t[2 * (t % 2) + half][:].rearrange("p (k s) -> p k s", s=P),
                        ACT.Copy).then_inc(ht_hi_done, 1)

            def split_w_hi(pair, slot):
                act.wait_ge(w_loaded[slot], 16 * (pair + 1))
                if not isinstance(pair, int) or pair >= 1:
                    act.wait_ge(summed, (2 * pair + slot - 1) * SB)
                nc.scalar.activation(w_hi[:, slot], w_raw[:, slot], ACT.Copy).then_inc(w_hi_done, 1)

            def split_first(n):
                split_o_hi(n % 2, n // 2, n % 4, n)

            def split_o_hi(slot, b, bank, count):
                act.wait_ge(summed, count + 1)
                nc.scalar.activation(o_hi[:, slot, b * BANK:(b + 1) * BANK], ps_o[bank][:],
                                     ACT.Copy).then_inc(o_hi_done, 1)

            square(0)
            for t in range(ST):
                if t + 1 < ST:
                    square(t + 1)
                if t in product_before_turn:
                    split_first(product_before_turn[t])
                split_ht_hi(t)
                if t == 2:
                    split_w_hi(0, 0)
                    split_w_hi(0, 1)
            for n in range(2 * SB - 3, 2 * SB):
                split_first(n)
            split_w_hi(1, 0)

            act.wait_ge(gate_step, 2)
            nc.scalar.activation(logs, gates, ACT.Abs).then_inc(log_step, 1)
            act.wait_ge(log_step, 1)
            nc.scalar.activation(logs, logs, ACT.Exp, scale=-1.0).then_inc(log_step, 1)
            act.wait_ge(log_step, 2)
            nc.scalar.activation(logs, logs, ACT.Ln, bias=1.0).then_inc(log_step, 1)

            def chunk(pair, slot, last=False):
                act.wait_ge(stored[slot], 32 * pair)
                for b in range(SB):
                    split_o_hi(slot, b, b, (2 * pair + slot) * SB + b)
                    if b == 0 and not last:
                        split_w_hi(pair + slot, 1 - slot)

            with act.Fori(1, PAIRS - 1) as i:
                chunk(i, 0)
                chunk(i, 1)
            chunk(PAIRS - 1, 0)
            chunk(PAIRS - 1, 1)
            chunk(PAIRS, 0, True)

        @block.vector
        def _(dve):
            def norm(t):
                dve.wait_ge(rooted, t + 1)
                if t == 0:
                    dve.wait_ge(const_in, 32)
                nc.vector.scalar_tensor_tensor(x_in[:, t % X_RING], x_in[:, t % X_RING], rstd[:, t:t + 1], gain[:],
                                               ALU.mult, ALU.mult).then_inc(normed, 1)

            def split_ht_lo(t):
                for half in range(2):
                    dve.wait_ge(ht_hi_done, 2 * t + half + 1)
                    k, s = slice(4 * half, 4 * half + 4), slice(t * P, (t + 1) * P)
                    nc.vector.tensor_tensor(
                        ht_lo[:, k, s], ps_t[2 * (t % 2) + half][:].rearrange("p (k s) -> p k s", s=P),
                        ht_hi[:, k, s].bitcast(F32), ALU.subtract).then_inc(ht_lo_done, 1)

            def split_w_lo(n, slot):
                dve.wait_ge(w_hi_done, n + 1)
                nc.vector.tensor_tensor(w_lo[:, slot], w_raw[:, slot], w_hi[:, slot].bitcast(F32),
                                        ALU.subtract).then_inc(w_lo_done, 1)

            def split_first(n):
                split_o_lo(n % 2, n // 2, n % 4, n)

            def split_o_lo(slot, b, bank, count):
                dve.wait_ge(o_hi_done, count + 1)
                s = slice(b * BANK, (b + 1) * BANK)
                nc.vector.tensor_tensor(o_lo[:, slot, s], ps_o[bank][:], o_hi[:, slot, s].bitcast(F32),
                                        ALU.subtract).then_inc(o_lo_done, 1)

            nc.vector.memset(mhalf[:], -0.5).then_inc(mhalf_set, 1)
            nc.vector.memset(ones[:], 1.0)
            nc.vector.memset(bias[:], 0.0).then_inc(bias_set, 1)
            norm(0)
            for t in range(ST):
                if t + 1 < ST:
                    norm(t + 1)
                if t in product_before_turn:
                    split_first(product_before_turn[t])
                split_ht_lo(t)
                if t == 2:
                    split_w_lo(0, 0)
                    split_w_lo(1, 1)
            for n in range(2 * SB - 3, 2 * SB):
                split_first(n)
            split_w_lo(2, 0)

            dve.wait_ge(o_lo_done, 2 * SB)
            nc.vector.tensor_tensor(gates, o_hi[GATES, 0].bitcast(F32), o_lo[GATES, 0].bitcast(F32),
                                    ALU.add).then_inc(gate_step, 1)
            dve.wait_ge(gate_step, 1)
            dve.wait_ge(bias_in, 16)
            nc.vector.tensor_scalar(gates, gates, bias[GATES], None, ALU.add).then_inc(gate_step, 1)
            dve.wait_ge(gate_step, 2)
            dve.wait_ge(log_step, 1)
            nc.vector.tensor_scalar(gates, gates, -1.0, 0.0, ALU.mult, ALU.max).then_inc(gate_step, 1)
            dve.wait_ge(gate_step, 3)
            dve.wait_ge(log_step, 3)
            nc.vector.tensor_tensor(gates, gates, logs, ALU.add).then_inc(gate_step, 1)
            dve.wait_ge(gate_step, 4)
            nc.vector.tensor_tensor_scan(logs, ones[GATES].to_broadcast([32, S]), gates, 0.0,
                                         ALU.mult, ALU.add).then_inc(gate_step, 1)
            dve.wait_ge(gate_step, 5)
            nc.vector.tensor_scalar(logs, logs, float(HEAD_DIM) ** 0.5, None, ALU.mult).then_inc(gate_step, 1)

            def chunk(pair, slot, last=False):
                n = 2 * pair + slot
                for b in range(SB):
                    split_o_lo(slot, b, b, n * SB + b)
                    if b == 0 and not last:
                        split_w_lo(n + 1, 1 - slot)

            with dve.Fori(1, PAIRS - 1) as i:
                chunk(i, 0)
                chunk(i, 1)
            chunk(PAIRS - 1, 0)
            chunk(PAIRS - 1, 1)
            chunk(PAIRS, 0, True)

        @block.tensor
        def _(pe):
            def turn(t):
                pe.wait_ge(normed, t + 1)
                if t == 0:
                    pe.wait_ge(const_in, 32)
                if t >= 2:
                    pe.wait_ge(ht_lo_done, 2 * (t - 1))
                for half in range(2):
                    for k in range(4):
                        last = nc.tensor.transpose(ps_t[2 * (t % 2) + half][:, k * P:(k + 1) * P],
                                                   x_in[:, t % X_RING, (4 * half + k) * P:(4 * half + k + 1) * P],
                                                   ident[:])
                    last.then_inc(turned, 1)

            def product(slot, b, bank):
                s = slice(b * BANK, (b + 1) * BANK)
                for k in range(DK):
                    for n, (w, h) in enumerate(((w_hi, ht_hi), (w_hi, ht_lo), (w_lo, ht_hi))):
                        last = nc.tensor.matmul(ps_o[bank][:], w[:, slot, k, :], h[:, k, s],
                                                start=(k == 0 and n == 0), stop=(k == DK - 1 and n == 2))
                last.then_inc(summed, 1)

            def product_first(n):
                slot, b = n % 2, n // 2
                pe.wait_ge(ht_lo_done, 2 * TPB * (b + 1))
                pe.wait_ge(w_lo_done, 2)
                if n >= 4:
                    pe.wait_ge(o_lo_done, n - 3)
                product(slot, b, n % 4)

            for t in range(ST):
                turn(t)
                if t in product_after_turn:
                    product_first(product_after_turn[t])
            for n in range(2 * SB - 2, 2 * SB):
                product_first(n)

            def chunk(pair, slot):
                n = 2 * pair + slot
                pe.wait_ge(w_lo_done, n + 1)
                for b in range(SB):
                    pe.wait_ge(o_lo_done, n * SB + b - 3)
                    product(slot, b, b)

            with pe.Fori(1, PAIRS - 1) as i:
                chunk(i, 0)
                chunk(i, 1)
            chunk(PAIRS - 1, 0)
            chunk(PAIRS - 1, 1)
            chunk(PAIRS, 0)


FLT_MAX = 3.4028234e38


def attend(nc, proj_hi, proj_lo, sinks, ident_dram, causal_dram, alibi_dram,
           decay, o_main, o_rest, rsum_inv):
    S = proj_hi.shape[1]
    QT = S // P
    QB = QT // 4
    DH = HEAD_DIM
    H = SWA_HEADS
    GROUP = SWA_HEADS // SWA_KV_HEADS
    KA = SWA_HEADS * DH
    VA = KA + SWA_KV_HEADS * DH
    QF = VA + SWA_KV_HEADS * DH
    KF = QF + FOX_HEADS * DH
    VF = KF + FOX_HEADS * DH
    SCALE = float(DH) ** -0.5
    assert SWA_HEADS == FOX_HEADS and QB == 4 and 2 * DH == P

    steps = [("swa", j) for j in range(QT // 2)] + [("fox", b, k) for b in range(QB) for k in range(4 * b + 4)]
    NSTEP = len(steps)
    BLOCK0 = [QT // 2 + 4 * (b * (b + 1) // 2) for b in range(QB)]
    fox_chunks = [[("fox", b, t, c) for t in range(4) for c in range(b + 1)] for b in range(QB)]
    swa_chunks = [("swa", j) for j in range(QT // 2)]
    chunk_at = [[] for _ in range(NSTEP)]
    for b, (start, span) in enumerate(((0, 3), (2, 6), (8, 7), (16, 12))):
        for n, c in enumerate(fox_chunks[b]):
            chunk_at[start + n * span // len(fox_chunks[b])].append(c)
    for n, c in enumerate(swa_chunks):
        chunk_at[30 + n * 9 // len(swa_chunks)].append(("next",) + c)
    turn_at = [[] for _ in range(NSTEP)]
    for g in range(4):
        turn_at[2 + g].append(("v", "fox", g))
        turn_at[42 + g].append(("v", "swa", g))
    turn_at[38].append(("r",))
    for i in range(NSTEP):
        turn_at[i].append(("p", (i + 2) % NSTEP) if i + 2 < NSTEP else ("next", "p", i + 2 - NSTEP))
    NCHUNK = len(swa_chunks) + sum(map(len, fox_chunks))
    NTURN = sum(map(len, turn_at))
    S_RING, T_RING, PT_RING, O_RING = 3, 3, 4, 4
    assert NCHUNK % S_RING == 0 and NTURN % T_RING == 0 and NSTEP % PT_RING == 0
    PRE_CHUNKS = len(swa_chunks)
    PRE_TURNS = [("v", "swa", g) for g in range(4)] + [("next", "p", 0), ("next", "p", 1)]
    turn_order = [g for at in turn_at for g in at]
    last_order = [g for g in turn_order if g[0] != "next" and g[:2] != ("v", "swa")]
    assert len(PRE_TURNS) % T_RING == 0
    BEFORE = -1

    def p_slot(kind, b=0):
        if kind == "swa":
            return 0, 0
        return (2, 2, 0, 1)[b], (0, 4 * BANK, 0, 0)[b]

    def width(b, t, c):
        return BANK if c < b else (t + 1) * P

    with ExitStack() as ctx:
        sb, pb, sem = scopes(nc, ctx)
        ident = sb("a_ident", [P, P])
        ident_r = sb("a_ident_r", [P, P], F32R)
        causal = sb("a_causal", [P, P])
        causal_r = sb("a_causal_r", [P, P], F32R)
        q_st = {k: sb(f"a_q_{k}", [P, S], F32R) for k in ("swa", "fox")}
        k_hi = {k: sb(f"a_k_hi_{k}", [P, S], F32R) for k in ("swa", "fox")}
        k_lo = {k: sb(f"a_k_lo_{k}", [P, S], F32R) for k in ("swa", "fox")}
        v_t = {k: sb(f"a_v_t_{k}", [P, S]) for k in ("swa", "fox")}
        v_st = {k: sb(f"a_v_{k}", [P, QT, P], F32R) for k in ("swa", "fox")}
        alibi = sb("a_alibi", [P, 2 * P])
        sink = sb("a_sink", [P, 1])
        sink_neg = sb("a_sink_neg", [P, 1])
        decay_sb = sb("a_decay", [P, S])
        probs = [sb(f"a_probs{i}", [P, 4 * keys]) for i, keys in enumerate((S, S, 3 * BANK))]
        neg_max = {"swa": sb("a_nm_swa", [P, QT]), "fox": sb("a_nm_fox", [P, QT, 4])}
        rsum = {k: sb(f"a_rsum_{k}", [P, QT]) for k in ("swa", "fox")}
        sink_exp = sb("a_sink_exp", [P, QT])
        recip = sb("a_recip", [P, 2 * QT])
        recip_t = sb("a_recip_t", [2 * QT, P])
        pt_hi = [sb(f"a_pt_hi{i}", [P, BANK], F32R) for i in range(PT_RING)]
        pt_lo = [sb(f"a_pt_lo{i}", [P, BANK], F32R) for i in range(PT_RING)]
        o_sb = [sb(f"a_o{i}", [P, BANK]) for i in range(O_RING)]
        ps_s = [pb(f"a_ps_s{i}") for i in range(S_RING)]
        ps_t = [pb(f"a_ps_t{i}") for i in range(T_RING)]
        ps_o = [pb(f"a_ps_o{i}") for i in range(2)]

        const_in = sem("a_const_in")
        const_r = sem("a_const_r")
        first_loaded = sem("a_first_loaded")
        qk_loaded = {k: sem(f"a_qk_loaded_{k}") for k in ("swa", "fox")}
        v_loaded = {k: sem(f"a_v_loaded_{k}") for k in ("swa", "fox")}
        sink_negated = sem("a_sink_negated")
        summed = sem("a_summed")
        scored = sem("a_scored")
        exped = sem("a_exped")
        turned = sem("a_turned")
        p_hi_done = sem("a_p_hi_done")
        p_lo_done = sem("a_p_lo_done")
        v_done = {k: sem(f"a_v_done_{k}") for k in ("swa", "fox")}
        weighted = sem("a_weighted")
        o_copied = sem("a_o_copied")
        o_stored = [sem(f"a_o_stored{i}") for i in range(O_RING)]
        sink_exped = sem("a_sink_exped")
        denom_done = sem("a_denom_done")
        recip_done = sem("a_recip_done")
        r_copied = sem("a_r_copied")
        r_stored = sem("a_r_stored")

        chunk_no, tile_no = {}, {}
        for i in range(NSTEP):
            for c in chunk_at[i]:
                chunk_no[c] = len(chunk_no)
                if c[0] == "fox" and c[3] == c[1]:
                    tile_no[("fox", c[1], c[2])] = len(tile_no)
                elif c[0] == "next":
                    tile_no[("next", "swa", 2 * c[2])] = len(tile_no)
                    tile_no[("next", "swa", 2 * c[2] + 1)] = len(tile_no)
        NTILE = len(tile_no)
        PRE_TILES = QT

        def chunk_count(h, c):
            n = chunk_no[c] if c in chunk_no else chunk_no[("next",) + c] - NCHUNK
            return h * NCHUNK + (PRE_CHUNKS + n + 1)

        def tile_count(h, t):
            n = tile_no[t] if t in tile_no else tile_no[("next",) + t] - NTILE
            return h * NTILE + (PRE_TILES + n + 1)

        def order_of(h):
            if isinstance(h, int) and h in (BEFORE, H - 1):
                return PRE_TURNS if h == BEFORE else last_order
            return turn_order

        def turn_count(h, g):
            before = 0 if h is BEFORE else h * NTURN + len(PRE_TURNS)
            return before + (order_of(h).index(g) + 1)

        def chunk_ring(c):
            n = chunk_no[c] if c in chunk_no else chunk_no[("next",) + c] - NCHUNK
            return (PRE_CHUNKS + n) % S_RING

        O_BLOCKS = 2 * QB

        def o_block(step):
            if step[0] == "swa":
                return step[1] // 2, step[1] % 2 == 0, step[1] % 2 == 1
            return QB + step[1], step[2] == 0, step[2] == 4 * step[1] + 3

        def p_cols(b, t, lo, hi):
            slot, at = p_slot("fox", b)
            row = at + t * BANK * (b + 1)
            return probs[slot][:, row + lo:row + hi]

        def swa_cols(t, lo, hi):
            return probs[0][:, t * 2 * P + lo:t * 2 * P + hi]

        def turn_width(step):
            if step[0] == "swa":
                return BANK
            return (4 - max(0, step[2] - 4 * step[1])) * P

        def turned_cols(i):
            if steps[i][0] == "swa":
                return (0 if i else P), BANK
            return 0, turn_width(steps[i])

        block = ctx.enter_context(nc.Block())

        @block.sync
        def _(sp):
            def load(dst, src, done):
                sp.dma_start(dst, src).then_inc(done, 16)

            def load_qk(kind, q0, k0, done, cols=slice(0, S)):
                for part, half in ((0, proj_hi), (1, proj_lo)):
                    rows = slice(part * DH, (part + 1) * DH)
                    load(q_st[kind][rows, cols].bitcast(F32), half[bass.ds(P + q0, DH), cols], done)
                    for dst, src in ((k_hi, proj_hi), (k_lo, proj_lo)):
                        load(dst[kind][rows, cols].bitcast(F32), src[bass.ds(P + k0, DH), cols], done)

            def load_v(kind, v0):
                for part, half in ((0, proj_hi), (1, proj_lo)):
                    load(v_t[kind][part * DH:(part + 1) * DH], half[bass.ds(P + v0, DH), :], v_loaded[kind])

            def load_bias(h, done):
                load(alibi[:], alibi_dram[bass.ds(h, 1)].rearrange("a p c -> (a p) c"), done)
                load(sink[:], sinks[0, bass.ds(h, 1)].partition_broadcast(P), done)

            def load_swa(h):
                load_qk("swa", h * DH, KA + (h // GROUP) * DH, qk_loaded["swa"])
                load_bias(h, qk_loaded["swa"])
                load_v("swa", VA + (h // GROUP) * DH)

            def load_fox(h):
                load_qk("fox", QF + h * DH, KF + h * DH, qk_loaded["fox"])
                load(decay_sb[:], decay[bass.ds(h, 1)].rearrange("a s -> (a s)").partition_broadcast(P),
                     qk_loaded["fox"])
                load_v("fox", VF + h * DH)

            for done in (*o_stored, r_stored):
                sp.sem_inc(done, 16)
            load_qk("swa", 0, KA, first_loaded, slice(0, S // 2))
            load_bias(0, first_loaded)
            sp.sem_inc(qk_loaded["swa"], 32)
            load_qk("swa", 0, KA, qk_loaded["swa"], slice(S // 2, S))
            load(ident[:], ident_dram, const_in)
            load(causal[:], causal_dram, const_in)
            load_v("swa", VA)
            load_fox(0)

            def store_outputs(h, n):
                sp.wait_ge(o_copied, h * O_BLOCKS + (n + 3))
                row = (n // QB) * KA + h * DH
                cols = slice((n % QB) * BANK, (n % QB + 1) * BANK)
                for part, dst in ((0, o_main), (1, o_rest)):
                    load(dst[bass.ds(row, DH), cols], o_sb[n % O_RING][part * DH:(part + 1) * DH], o_stored[n % O_RING])

            def turn(h, last=False):
                if not last:
                    sp.wait_ge(scored, chunk_count(h, ("swa", QT // 2 - 1)))
                    sp.wait_ge(v_done["swa"], 4 * (h + 1))
                    sp.wait_ge(sink_exped, h + 1)
                    load_swa(h + 1)
                for n in range(QB + 2):
                    store_outputs(h, n)
                if not last:
                    sp.wait_ge(scored, chunk_count(h, ("fox", 3, 3, 3)))
                    sp.wait_ge(v_done["fox"], 4 * (h + 1))
                    load_fox(h + 1)
                store_outputs(h, QB + 2)
                sp.wait_ge(r_copied, h + 2)
                for part in range(2):
                    load(rsum_inv[bass.ds(part * H + h, 1)].rearrange("a (t q) -> (a t) q", q=P),
                         recip_t[part * QT:(part + 1) * QT], r_stored)
                store_outputs(h, QB + 3)

            with sp.Fori(0, H - 1) as h:
                turn(h)
            turn(H - 1, True)
            for done in o_stored:
                sp.wait_ge(done, 16 + 32 * H * O_BLOCKS // O_RING)
            sp.wait_ge(r_stored, 16 + 32 * H)

        @block.tensor
        def _(pe):
            def scores(h, c):
                ring = chunk_ring(c)
                if not (h is BEFORE and c[2] < S_RING):
                    pe.wait_ge(scored, chunk_count(h, c) - S_RING)
                kind = c[1] if c[0] == "next" else c[0]
                if kind == "swa":
                    j = c[2]
                    if h is BEFORE and j == 0:
                        pe.wait_ge(first_loaded, 128)
                    elif j == (QT // 4 if h is BEFORE else 0):
                        pe.wait_ge(qk_loaded["swa"], (h + 1) * 128 + 128)
                    for n in range(2):
                        t = 2 * j + n
                        lo = 0 if t else P
                        out = ps_s[ring][:, n * 2 * P + lo:(n + 1) * 2 * P]
                        for m, kk in enumerate((k_hi, k_lo)):
                            last = nc.tensor.matmul(out, q_st[kind][:, t * P:(t + 1) * P],
                                                    kk[kind][:, (t - 1) * P + lo:(t + 1) * P],
                                                    start=(m == 0), stop=(m == 1))
                else:
                    _, b, t, n = c
                    if (b, t, n) == (0, 0, 0):
                        pe.wait_ge(qk_loaded["fox"], h * 112 + 112)
                    w = width(b, t, n)
                    q = slice((4 * b + t) * P, (4 * b + t + 1) * P)
                    for m, kk in enumerate((k_hi, k_lo)):
                        last = nc.tensor.matmul(ps_s[ring][:, 0:w], q_st[kind][:, q],
                                                kk[kind][:, n * BANK:n * BANK + w],
                                                start=(m == 0), stop=(m == 1 and n < b))
                    if n == b:
                        last = nc.tensor.matmul(ps_s[ring][:, w - P:w], ident_r[:], causal_r[:],
                                                start=False, stop=True)
                last.then_inc(summed, 1)

            def wait_bank_read(h, g):
                what = g[1:] if g[0] == "next" else g
                if what[0] == "v":
                    head = h + 1 if what[1] == "swa" else h
                    pe.wait_ge(v_done[what[1]], 4 * head + what[2] + 1)
                elif what[0] == "r":
                    pe.wait_ge(r_copied, h + 2)
                else:
                    head = h + 1 if g[0] == "next" else h
                    pe.wait_ge(p_lo_done, head * NSTEP + what[1] + 2)

            def turn_over(h, g):
                order = order_of(h)
                n = order.index(g)
                ring = n % T_RING
                if n >= T_RING:
                    wait_bank_read(h, order[n - T_RING])
                elif h is not BEFORE:
                    wait_bank_read(h - 1, turn_order[n - T_RING])
                    if n == 0:
                        pe.wait_ge(v_done["swa"], 4 * h + 4)
                what = g[1:] if g[0] == "next" else g
                bank = ps_t[ring]
                if what[0] == "v":
                    kind = what[1]
                    if what[2] == 0:
                        pe.wait_ge(v_loaded[kind], 32 * ((h + 1 if kind == "swa" else h) + 1))
                        if h is BEFORE:
                            pe.wait_ge(const_in, 32)
                    for m in range(4):
                        k = 4 * what[2] + m
                        last = nc.tensor.transpose(bank[:, m * P:(m + 1) * P],
                                                   v_t[kind][:, k * P:(k + 1) * P], ident[:])
                elif what[0] == "r":
                    pe.wait_ge(recip_done, 2 * h + 3)
                    last = nc.tensor.transpose(bank[0:2 * QT, 0:P], recip[:], ident[:])
                else:
                    step = steps[what[1]]
                    if step[0] == "swa":
                        j = step[1]
                        pe.wait_ge(exped, tile_count(h + 1 if g[0] == "next" else h, ("swa", 2 * j + 1)))
                        for m, (q, half) in enumerate(((2 * j, 0), (2 * j, 1), (2 * j + 1, 0), (2 * j + 1, 1))):
                            if (q, half) == (0, 0):
                                continue
                            last = nc.tensor.transpose(bank[:, m * P:(m + 1) * P],
                                                       swa_cols(q, half * P, (half + 1) * P), ident[:])
                    else:
                        _, b, k = step
                        if k == 0:
                            pe.wait_ge(exped, tile_count(h, ("fox", b, 3)))
                        first = max(0, k - 4 * b)
                        for m, t in enumerate(range(first, 4)):
                            last = nc.tensor.transpose(bank[:, m * P:(m + 1) * P],
                                                       p_cols(b, t, k * P, (k + 1) * P), ident[:])
                last.then_inc(turned, 1)

            def weigh(h, i):
                step = steps[i]
                kind = step[0]
                n, first, last_one = o_block(step)
                pe.wait_ge(p_lo_done, h * NSTEP + i + 2)
                if kind == "swa" and i == 0:
                    pe.wait_ge(v_done["swa"], h * 4 + 4)
                if kind == "fox" and i == BLOCK0[0]:
                    pe.wait_ge(v_done["fox"], h * 4 + 4)
                if first:
                    pe.wait_ge(o_copied, h * O_BLOCKS + n + 1)
                bank, hi, lo = ps_o[n % 2], pt_hi[i % PT_RING], pt_lo[i % PT_RING]
                if kind == "swa":
                    t, at = 2 * step[1], (step[1] % 2) * 2 * P
                    parts = [(t, P, 3 * P, 0, 2 * P), (t - 1, 0, P, 0, P), (t + 1, 3 * P, 4 * P, P, 2 * P)]
                    parts = [x for x in parts if x[0] >= 0]
                    for m, (k, c0, c1, o0, o1) in enumerate(parts):
                        for pt in (hi, lo):
                            last = nc.tensor.matmul(bank[:, at + o0:at + o1], v_st[kind][:, k], pt[:, c0:c1],
                                                    start=(m == 0 and pt is hi),
                                                    stop=(m == len(parts) - 1 and pt is lo),
                                                    skip_group_check=True)
                else:
                    w = turn_width(step)
                    for pt in (hi, lo):
                        last = nc.tensor.matmul(bank[:, BANK - w:BANK], v_st[kind][:, step[2]], pt[:, 0:w],
                                                start=(first and pt is hi), stop=(last_one and pt is lo),
                                                skip_group_check=True)
                last.then_inc(weighted, 1)

            pe.sem_inc(weighted, 1)
            for c in swa_chunks:
                scores(BEFORE, ("next",) + c)
            for g in PRE_TURNS:
                turn_over(BEFORE, g)
            pe.wait_ge(const_r, 2)

            def turn(h, last=False):
                for i in range(NSTEP):
                    for c in chunk_at[i]:
                        if not (last and c[0] == "next"):
                            scores(h, c)
                    for g in turn_at[i]:
                        if not (last and (g[0] == "next" or g[:2] == ("v", "swa"))):
                            turn_over(h, g)
                    weigh(h, i)

            with pe.Fori(0, H - 1) as h:
                turn(h)
            turn(H - 1, True)

        @block.vector
        def _(dve):
            def score(h, c):
                ring = chunk_ring(c)
                kind = c[1] if c[0] == "next" else c[0]
                dve.wait_ge(summed, chunk_count(h, c))
                if kind == "swa":
                    j = c[2]
                    if j == 0:
                        if h is BEFORE:
                            dve.wait_ge(first_loaded, 128)
                        else:
                            dve.wait_ge(qk_loaded["swa"], 128 * (h + 1) + 128)
                        nc.vector.tensor_scalar(sink_neg[:], sink[:], -1.0, None, ALU.mult).then_inc(sink_negated, 1)
                        dve.wait_ge(sink_negated, h + 2)
                        if h is not BEFORE:
                            dve.wait_ge(turned, turn_count(h, ("p", BLOCK0[3] - 1)))
                            dve.wait_ge(sink_exped, h + 1)
                    nc.vector.nop(nofuse=True)
                    for n in range(2):
                        t = 2 * j + n
                        lo = 0 if t else P
                        last = nc.vector.tensor_tensor_reduce(
                            out=swa_cols(t, lo, 2 * P), in0=ps_s[ring][:, n * 2 * P + lo:(n + 1) * 2 * P],
                            in1=alibi[:, lo:], scale=-SCALE, scalar=sink_neg[:], op0=ALU.add, op1=ALU.min,
                            accum_out=neg_max["swa"][:, t:t + 1])
                else:
                    _, b, t, n = c
                    if (b, t, n) == (0, 0, 0):
                        dve.wait_ge(qk_loaded["fox"], 112 * h + 112)
                        dve.wait_ge(turned, turn_count(h - 1, ("p", NSTEP - 1)))
                    if (b, t, n) == (2, 0, 0):
                        dve.wait_ge(turned, turn_count(h, ("p", QT // 2 - 1)))
                    w = width(b, t, n)
                    nm = neg_max["fox"][:, 4 * b + t]
                    if n:
                        dve.wait_ge(scored, chunk_count(h, c) - 1)
                    nc.vector.nop(nofuse=True)
                    last = nc.vector.tensor_tensor_reduce(
                        out=p_cols(b, t, n * BANK, n * BANK + w), in0=ps_s[ring][:, 0:w],
                        in1=decay_sb[:, n * BANK:n * BANK + w], scale=-SCALE,
                        scalar=nm[:, n - 1:n] if n else FLT_MAX, op0=ALU.add, op1=ALU.min,
                        accum_out=nm[:, n:n + 1])
                last.then_inc(scored, 1)

            def copy_out(h, g):
                bank = ps_t[order_of(h).index(g) % T_RING]
                what = g[1:] if g[0] == "next" else g
                if what[0] == "p":
                    head, i = (h + 1 if g[0] == "next" else h), what[1]
                    lo, hi = turned_cols(i)
                    dve.wait_ge(p_hi_done, head * NSTEP + i + 1)
                    nc.vector.tensor_tensor(pt_lo[i % PT_RING][:, lo:hi], bank[:, lo:hi],
                                            pt_hi[i % PT_RING][:, lo:hi].bitcast(F32),
                                            ALU.subtract).then_inc(p_lo_done, 1)
                elif what[0] == "v":
                    pass
                else:
                    dve.wait_ge(turned, turn_count(h, g))
                    dve.wait_ge(r_stored, 16 + 32 * h)
                    nc.vector.tensor_copy(recip_t[:], bank[0:2 * QT, 0:P]).then_inc(r_copied, 1)

            def invert_swa(h):
                dve.wait_ge(sink_exped, h + 1)
                dve.wait_ge(r_copied, h + 1)
                nc.vector.tensor_tensor(sink_exp[:], sink_exp[:], rsum["swa"][:], ALU.add).then_inc(denom_done, 1)
                dve.wait_ge(denom_done, h + 1)
                nc.vector.reciprocal(recip[:, 0:QT], sink_exp[:]).then_inc(recip_done, 1)

            def invert_fox(h):
                dve.wait_ge(exped, tile_count(h, ("fox", QB - 1, 3)))
                nc.vector.reciprocal(recip[:, QT:2 * QT], rsum["fox"][:]).then_inc(recip_done, 1)

            for done in (recip_done, r_copied, p_lo_done):
                dve.sem_inc(done, 1)
            for c in swa_chunks:
                score(BEFORE, ("next",) + c)
            dve.wait_ge(const_in, 32)
            nc.vector.tensor_copy(ident_r[:], ident[:]).then_inc(const_r, 1)
            nc.vector.tensor_copy(causal_r[:], causal[:]).then_inc(const_r, 1)
            for g in PRE_TURNS:
                copy_out(BEFORE, g)

            def turn(h, last=False):
                for i in range(NSTEP):
                    for c in chunk_at[i]:
                        if not (last and c[0] == "next"):
                            score(h, c)
                    if i == 4:
                        invert_swa(h)
                    if i == 36:
                        invert_fox(h)
                    for g in turn_at[i]:
                        if not (last and (g[0] == "next" or g[:2] == ("v", "swa"))):
                            copy_out(h, g)

            with dve.Fori(0, H - 1) as h:
                turn(h)
            turn(H - 1, True)

        @block.scalar
        def _(act):
            def exponentiate(h, c):
                if c[0] == "next":
                    if c[2] == 0 and h is not BEFORE:
                        act.wait_ge(recip_done, 2 * h + 2)
                    act.wait_ge(scored, chunk_count(h, c))
                    for t in (2 * c[2], 2 * c[2] + 1):
                        cols = swa_cols(t, 0 if t else P, 2 * P)
                        nc.scalar.activation(cols, cols, ACT.Exp, scale=-1.0, bias=neg_max["swa"][:, t:t + 1],
                                             accum_out=rsum["swa"][:, t:t + 1]).then_inc(exped, 1)
                elif c[3] == c[1]:
                    _, b, t, _ = c
                    if (b, t) == (0, 0):
                        act.wait_ge(recip_done, 2 * h + 1)
                    act.wait_ge(scored, chunk_count(h, c))
                    cols = p_cols(b, t, 0, (4 * b + t + 1) * P)
                    nc.scalar.activation(cols, cols, ACT.Exp, scale=-1.0, bias=neg_max["fox"][:, 4 * b + t, b:b + 1],
                                         accum_out=rsum["fox"][:, 4 * b + t:4 * b + t + 1]).then_inc(exped, 1)

            def copy_hi(h, g):
                what = g[1:] if g[0] == "next" else g
                bank = ps_t[order_of(h).index(g) % T_RING]
                if what[0] == "r":
                    return
                if what[0] == "v":
                    kind, m = what[1:]
                    act.wait_ge(turned, turn_count(h, g))
                    if m == 0 and h is not BEFORE:
                        act.wait_ge(weighted, h * NSTEP + (QT // 2 if kind == "swa" else 0) + 1)
                    nc.scalar.activation(v_st[kind][:, 4 * m:4 * m + 4],
                                         bank[:].rearrange("p (k d) -> p k d", d=P), ACT.Copy).then_inc(v_done[kind], 1)
                    return
                head, i = (h + 1 if g[0] == "next" else h), what[1]
                lo, hi = turned_cols(i)
                act.wait_ge(turned, turn_count(h, g))
                if h is not BEFORE:
                    act.wait_ge(weighted, head * NSTEP + i - PT_RING + 2)
                nc.scalar.activation(pt_hi[i % PT_RING][:, lo:hi], bank[:, lo:hi], ACT.Copy).then_inc(p_hi_done, 1)

            def copy_outputs(h, i):
                n, _, last_one = o_block(steps[i])
                if last_one:
                    act.wait_ge(weighted, h * NSTEP + i + 2)
                    act.wait_ge(o_stored[n % O_RING], 16 + 32 * (h * (O_BLOCKS // O_RING) + n // O_RING))
                    nc.scalar.activation(o_sb[n % O_RING][:], ps_o[n % 2][:], ACT.Copy).then_inc(o_copied, 1)

            def weigh_sinks(h):
                act.wait_ge(scored, chunk_count(h, ("swa", QT // 2 - 1)))
                act.wait_ge(recip_done, 2 * h + 1)
                nc.scalar.activation(sink_exp[:], neg_max["swa"][:], ACT.Exp, bias=sink[:]).then_inc(sink_exped, 1)

            act.sem_inc(o_copied, 2)
            for c in swa_chunks:
                exponentiate(BEFORE, ("next",) + c)
            for g in PRE_TURNS:
                copy_hi(BEFORE, g)

            def turn(h, last=False):
                for i in range(NSTEP):
                    for g in turn_at[i]:
                        if not (last and (g[0] == "next" or g[:2] == ("v", "swa"))):
                            copy_hi(h, g)
                    for c in chunk_at[i - 1] if i else []:
                        if not (last and c[0] == "next"):
                            exponentiate(h, c)
                    if i == 2:
                        weigh_sinks(h)
                    if i:
                        copy_outputs(h, i - 1)
                copy_outputs(h, NSTEP - 1)

            with act.Fori(0, H - 1) as h:
                turn(h)
            turn(H - 1, True)


def tables():
    import numpy as np

    scale = float(HEAD_DIM) ** -0.5
    q, k = np.arange(P)[:, None], np.arange(P)[None, :]
    causal = np.where(k > q, NEG, 0.0).astype(np.float32)
    k = np.arange(2 * P)[None, :] - P
    band = (k // CHUNK <= q // CHUNK) & (k // CHUNK >= q // CHUNK - 1)
    slopes = 2.0 ** (-8.0 * np.arange(1, SWA_HEADS + 1) / SWA_HEADS)
    alibi = np.where(band, -slopes[:, None, None] * np.abs(q - k) / scale, NEG).astype(np.float32)
    return causal, alibi


MLP_TOKENS = 1024
MLP_CHUNK = 256


def mix_out(nc, o_main, o_rest, rsum_inv, w_out, x, norm_mlp, w_up, ident_dram, h_hi, h_lo, wu_raw,
            x_mid, h_hi_dram, h_lo_dram):
    E, S = o_main.shape
    D = w_out.shape[1]
    EK, DK, ST = E // P, D // P, S // P
    HALVES = D // BANK
    PAIRS = ST // 2
    KEPT = MLP_TOKENS // P
    BLOCK = KEPT // 2
    assert PAIRS == 2 * BLOCK and EK == 8 and DK * MLP_CHUNK == 2 * D
    with ExitStack() as ctx:
        sb, pb, sem = scopes(nc, ctx)
        ident = sb("m_ident", [P, P])
        gain = sb("m_gain", [P, D])
        mhalf = sb("m_mhalf", [P, 1])
        w_hi = sb("m_w_hi", [P, EK, D], F32R)
        w_lo = sb("m_w_lo", [P, EK, D], F32R)
        mix = sb("m_mix", [P, 2, EK, P])
        rest = sb("m_rest", [P, 2, EK, P])
        inv = sb("m_inv", [P, 2, EK, P])
        mix_hi = sb("m_mix_hi", [P, 2, EK, P], F32R)
        mix_lo = sb("m_mix_lo", [P, 2, EK, P], F32R)
        x_in = sb("m_x_in", [P, 2, D])
        xm = sb("m_xm", [P, 2, D])
        xn = sb("m_xn", [P, 2, D])
        w_raw = [room[:, slot] for room in (x_in, xm, xn, wu_raw[:].rearrange("p (r a) c -> p r (a c)", r=2))
                 for slot in range(2)]
        ssum = sb("m_ssum", [P, 2])
        rstd = sb("m_rstd", [P, 2])
        ps_o = [pb(f"m_ps_o{i}") for i in range(4)]
        ps_t = [pb(f"m_ps_t{i}") for i in range(4)]

        const_in = sem("m_const_in")
        w_loaded = [sem(f"m_w_loaded{k}") for k in range(EK)]
        up_loaded = sem("m_up_loaded")
        w_hi_done = sem("m_w_hi_done")
        w_lo_done = sem("m_w_lo_done")
        o_loaded = [sem(f"m_o_loaded{i}") for i in range(2)]
        x_loaded = [sem(f"m_x_loaded{i}") for i in range(2)]
        mhalf_set = sem("m_mhalf_set")
        joined = sem("m_joined")
        divided = sem("m_divided")
        mix_hi_done = sem("m_mix_hi_done")
        mix_lo_done = sem("m_mix_lo_done")
        summed = sem("m_summed")
        added = sem("m_added")
        x_stored = [sem(f"m_x_stored{i}") for i in range(2)]
        squared = sem("m_squared")
        meaned = sem("m_meaned")
        rooted = sem("m_rooted")
        normed = sem("m_normed")
        turned = sem("m_turned")
        ht_hi_done = sem("m_ht_hi_done")
        ht_lo_done = sem("m_ht_lo_done")
        ht_stored = sem("m_ht_stored")

        block = ctx.enter_context(nc.Block())

        def walk(eng, tile):
            for start, end in ((0, BLOCK), (BLOCK, PAIRS - 1)):
                tile(start, 0, (KEPT - 1) * P, start == 0)
                tile(start, 1, 0, start == 0)
                with eng.Fori(start + 1, end) as i:
                    tile(i, 0, (2 * (i - start) - 1) * P, start == 0)
                    tile(i, 1, 2 * (i - start) * P, start == 0)
            tile(PAIRS - 1, 0, (KEPT - 3) * P, False)
            tile(PAIRS - 1, 1, (KEPT - 2) * P, False)

        def is_first(pair, slot):
            return isinstance(pair, int) and (pair, slot) == (0, 0)

        def is_last(pair, slot):
            return isinstance(pair, int) and (pair, slot) == (PAIRS - 1, 1)

        def in_first_pair(pair):
            return isinstance(pair, int) and pair == 0

        @block.sync
        def _(sp):
            def load_mix(pair, slot):
                t = 2 * pair + slot
                s = bass.ds(t * P, P)
                if not in_first_pair(pair):
                    sp.wait_ge(mix_lo_done, t - 1)
                    sp.nop(nofuse=True)
                done = o_loaded[slot]
                sp.dma_start(mix[:, slot], o_main[:, s].rearrange("(k p) s -> p k s", p=P)).then_inc(done, 16)
                sp.dma_start(rest[:, slot], o_rest[:, s].rearrange("(k p) s -> p k s", p=P)).then_inc(done, 16)
                for half in range(2):
                    rows = slice(half * HEAD_DIM, (half + 1) * HEAD_DIM)
                    src = rsum_inv[:, s].rearrange("(k two) s -> two k s", two=2)[half]
                    sp.dma_start(inv[rows, slot], src.partition_broadcast(HEAD_DIM)).then_inc(done, 16)

            def load_x(pair, slot):
                t = 2 * pair + slot
                if not in_first_pair(pair):
                    sp.wait_ge(added, 2 * (t - 1))
                    sp.nop(nofuse=True)
                sp.dma_start(x_in[:, slot], x[bass.ds(t * P, P), :]).then_inc(x_loaded[slot], 16)

            def store_ht(pair):
                sp.wait_ge(ht_lo_done, 4 * pair + 4)
                sp.nop(nofuse=True)
                cols = bass.ds(2 * pair * P, 2 * P)
                for part, dst in ((h_hi, h_hi_dram), (h_lo, h_lo_dram)):
                    sp.dma_start(dst[:, cols].rearrange("(k p) s -> p k s", p=P),
                                 part[:, :, cols].bitcast(F32)).then_inc(ht_stored, 16)

            load_mix(0, 0)
            for k in range(EK):
                sp.dma_start(w_raw[k], w_out[k * P:(k + 1) * P, :]).then_inc(w_loaded[k], 16)
            sp.dma_start(ident[:], ident_dram).then_inc(const_in, 16)
            sp.dma_start(gain[:], norm_mlp[0].partition_broadcast(P)).then_inc(const_in, 16)
            load_mix(0, 1)
            sp.wait_ge(w_lo_done, 2)
            load_x(0, 0)
            load_x(0, 1)
            sp.wait_ge(w_lo_done, EK)
            sp.dma_start(wu_raw[:], w_up.rearrange("(k p) f -> p k f", p=P)[:, :, 0:MLP_CHUNK]).then_inc(up_loaded, 16)

            def tile(pair, slot, at, first_block):
                t = 2 * pair + slot
                ends = isinstance(pair, int) and pair == PAIRS - 1
                if not ends:
                    load_mix(pair + 1, slot)
                sp.wait_ge(added, 2 * t + 2)
                sp.nop(nofuse=True)
                sp.dma_start(x_mid[bass.ds(t * P, P), :], xm[:, slot]).then_inc(x_stored[slot], 16)
                if not ends:
                    load_x(pair + 1, slot)
                if slot == 0 and not is_first(pair, slot) and (first_block or isinstance(pair, int) and pair == BLOCK):
                    store_ht(pair - 1)

            walk(sp, tile)
            for slot in range(2):
                sp.wait_ge(x_stored[slot], 16 * PAIRS)
            sp.wait_ge(ht_stored, 32 * BLOCK)
            sp.wait_ge(up_loaded, 16)

        @block.gpsimd
        def _(pool):
            def join(pair, slot):
                pool.wait_ge(o_loaded[slot], 64 * (pair + 1))
                nc.gpsimd.tensor_tensor(mix[:, slot], mix[:, slot], rest[:, slot], ALU.add).then_inc(joined, 1)

            join(0, 0)
            pool.wait_ge(mhalf_set, 1)

            def tile(pair, slot, at, first_block):
                t = 2 * pair + slot
                if not is_last(pair, slot):
                    join(pair + slot, 1 - slot)
                pool.wait_ge(squared, t + 1)
                nc.gpsimd.nop(nofuse=True)
                nc.gpsimd.tensor_scalar(rstd[:, slot:slot + 1], ssum[:, slot:slot + 1], 1.0 / D, EPS,
                                        ALU.mult, ALU.add).then_inc(meaned, 1)
                pool.wait_ge(meaned, t + 1)
                nc.gpsimd.tensor_tensor(rstd[:, slot:slot + 1], rstd[:, slot:slot + 1], mhalf[:],
                                        ALU.pow).then_inc(rooted, 1)

            walk(pool, tile)

        @block.scalar
        def _(act):
            def split_mix(pair, slot):
                t = 2 * pair + slot
                act.wait_ge(divided, t + 1)
                if not in_first_pair(pair):
                    act.wait_ge(summed, HALVES * (t - 1))
                nc.scalar.activation(mix_hi[:, slot], mix[:, slot], ACT.Copy).then_inc(mix_hi_done, 1)

            def split_ht(pair, slot, at):
                t = 2 * pair + slot
                if isinstance(pair, int) and (pair, slot) == (BLOCK, 0):
                    act.wait_ge(ht_stored, 32 * BLOCK)
                for half in range(2):
                    act.wait_ge(turned, 2 * t + half + 1)
                    nc.scalar.activation(h_hi[:, 4 * half:4 * half + 4, bass.ds(at, P)],
                                         ps_t[2 * slot + half][:].rearrange("p (k s) -> p k s", s=P),
                                         ACT.Copy).then_inc(ht_hi_done, 1)

            split_mix(0, 0)
            for k in range(EK):
                act.wait_ge(w_loaded[k], 16)
                nc.scalar.activation(w_hi[:, k], w_raw[k], ACT.Copy).then_inc(w_hi_done, 1)

            def tile(pair, slot, at, first_block):
                t = 2 * pair + slot
                if not is_last(pair, slot):
                    split_mix(pair + slot, 1 - slot)
                act.wait_ge(added, 2 * t + 2)
                if not in_first_pair(pair):
                    act.wait_ge(turned, 2 * (t - 1))
                nc.scalar.activation(xn[:, slot], xm[:, slot], ACT.Square,
                                     accum_out=ssum[:, slot:slot + 1]).then_inc(squared, 1)
                if not is_first(pair, slot):
                    split_ht(pair - 1 + slot, 1 - slot, at)

            walk(act, tile)
            split_ht(PAIRS - 1, 1, (KEPT - 1) * P)

        @block.vector
        def _(dve):
            def divide(pair, slot):
                dve.wait_ge(joined, 2 * pair + slot + 1)
                nc.vector.tensor_tensor(mix[:, slot], mix[:, slot], inv[:, slot], ALU.mult).then_inc(divided, 1)

            def split_mix(pair, slot):
                dve.wait_ge(mix_hi_done, 2 * pair + slot + 1)
                nc.vector.tensor_tensor(mix_lo[:, slot], mix[:, slot], mix_hi[:, slot].bitcast(F32),
                                        ALU.subtract).then_inc(mix_lo_done, 1)

            def split_ht(pair, slot, at):
                t = 2 * pair + slot
                for half in range(2):
                    k, s = slice(4 * half, 4 * half + 4), bass.ds(at, P)
                    dve.wait_ge(ht_hi_done, 2 * t + half + 1)
                    nc.vector.tensor_tensor(h_lo[:, k, s],
                                            ps_t[2 * slot + half][:].rearrange("p (k s) -> p k s", s=P),
                                            h_hi[:, k, s].bitcast(F32), ALU.subtract).then_inc(ht_lo_done, 1)

            nc.vector.memset(mhalf[:], -0.5).then_inc(mhalf_set, 1)
            divide(0, 0)
            split_mix(0, 0)
            for k in range(EK):
                dve.wait_ge(w_hi_done, k + 1)
                nc.vector.tensor_tensor(w_lo[:, k], w_raw[k], w_hi[:, k].bitcast(F32),
                                        ALU.subtract).then_inc(w_lo_done, 1)

            def tile(pair, slot, at, first_block):
                t = 2 * pair + slot
                if not is_last(pair, slot):
                    divide(pair + slot, 1 - slot)
                    split_mix(pair + slot, 1 - slot)
                dve.wait_ge(x_loaded[slot], 16 * (pair + 1))
                dve.wait_ge(x_stored[slot], 16 * pair)
                for half in range(HALVES):
                    cols = slice(half * BANK, (half + 1) * BANK)
                    dve.wait_ge(summed, HALVES * t + half + 1)
                    nc.vector.tensor_tensor(xm[:, slot, cols], ps_o[2 * slot + half][:], x_in[:, slot, cols],
                                            ALU.add).then_inc(added, 1)
                if not is_first(pair, slot):
                    split_ht(pair - 1 + slot, 1 - slot, at)
                else:
                    dve.wait_ge(const_in, 32)
                dve.wait_ge(rooted, t + 1)
                nc.vector.scalar_tensor_tensor(xn[:, slot], xm[:, slot], rstd[:, slot:slot + 1], gain[:],
                                               ALU.mult, ALU.mult).then_inc(normed, 1)

            walk(dve, tile)
            split_ht(PAIRS - 1, 1, (KEPT - 1) * P)

        @block.tensor
        def _(pe):
            def turn(pair, slot):
                t = 2 * pair + slot
                pe.wait_ge(normed, t + 1)
                if not in_first_pair(pair):
                    pe.wait_ge(ht_lo_done, 2 * (t - 1))
                for half in range(2):
                    for k in range(4):
                        col = (4 * half + k) * P
                        last = nc.tensor.transpose(ps_t[2 * slot + half][:, k * P:(k + 1) * P],
                                                   xn[:, slot, col:col + P], ident[:])
                    last.then_inc(turned, 1)

            def tile(pair, slot, at, first_block):
                t = 2 * pair + slot
                pe.wait_ge(mix_lo_done, t + 1)
                order = [(half, k) for half in range(HALVES) for k in range(EK)]
                if is_first(pair, slot):
                    order = [(half, k) for k in range(EK) for half in range(HALVES)]
                for half, k in order:
                    if k == 0 and not in_first_pair(pair):
                        pe.wait_ge(added, HALVES * t - 3 + half)
                    if is_first(pair, slot) and half == 0:
                        pe.wait_ge(w_lo_done, k + 1)
                    cols = slice(half * BANK, (half + 1) * BANK)
                    for n, (m, w) in enumerate(((mix_hi, w_hi), (mix_hi, w_lo), (mix_lo, w_hi))):
                        last = nc.tensor.matmul(ps_o[2 * slot + half][:], m[:, slot, k], w[:, k, cols],
                                                start=(k == 0 and n == 0), stop=(k == EK - 1 and n == 2))
                    if k == EK - 1:
                        last.then_inc(summed, 1)
                if is_first(pair, slot):
                    pe.wait_ge(const_in, 32)
                else:
                    turn(pair - 1 + slot, 1 - slot)

            walk(pe, tile)
            turn(PAIRS - 1, 1)


def mlp(nc, x_mid, h_hi, h_lo, wu_raw, h_hi_dram, h_lo_dram, w_up, w_down, norm_final, out):
    S, D = x_mid.shape
    F = w_up.shape[1]
    DK = D // P
    T, C = MLP_TOKENS, MLP_CHUNK
    NB, NC = S // T, F // C
    FT, SBK, ST, HALVES = C // P, T // BANK, T // P, D // BANK
    UPS = FT * SBK
    DOWNS = ST * HALVES
    RING = 4
    with ExitStack() as ctx:
        sb, pb, sem = scopes(nc, ctx)
        gain = sb("f_gain", [P, D])
        mhalf = sb("f_mhalf", [P, 1])
        acc = sb("f_acc", [P, ST, D])
        u_hi = [sb(f"f_u_hi{i}", [P, FT, T], F32R) for i in range(2)]
        u_lo = [sb(f"f_u_lo{i}", [P, FT, T], F32R) for i in range(2)]
        wu_hi = sb("f_wu_hi", [P, DK, C], F32R)
        wu_lo = sb("f_wu_lo", [P, DK, C], F32R)
        wd_raw = sb("f_wd_raw", [P, FT, D])
        wd_hi = sb("f_wd_hi", [P, FT, D], F32R)
        wd_lo = sb("f_wd_lo", [P, FT, D], F32R)
        r = sb("f_r", [P, 2, BANK])
        sq = sb("f_sq", [P, 2, BANK])
        y = sb("f_y", [P, 2, D])
        ssum = sb("f_ssum", [P, 2])
        rstd = sb("f_rstd", [P, 2])
        ps_u = [pb(f"f_ps_u{i}") for i in range(RING)]
        ps_d = [pb(f"f_ps_d{i}") for i in range(RING)]

        const_in = sem("f_const_in")
        mhalf_set = sem("f_mhalf_set")
        h_loaded = [sem(f"f_h_loaded{i}") for i in range(SBK)]
        acc_loaded = sem("f_acc_loaded")
        wu_loaded = sem("f_wu_loaded")
        wu_hi_done = sem("f_wu_hi_done")
        wu_lo_done = sem("f_wu_lo_done")
        wd_loaded = sem("f_wd_loaded")
        wd_hi_done = sem("f_wd_hi_done")
        wd_lo_done = sem("f_wd_lo_done")
        upped = sem("f_upped")
        relu_done = sem("f_relu_done")
        sq_done = sem("f_sq_done")
        u_hi_done = sem("f_u_hi_done")
        u_lo_done = sem("f_u_lo_done")
        downed = sem("f_downed")
        added = sem("f_added")
        squared = sem("f_squared")
        meaned = sem("f_meaned")
        rooted = sem("f_rooted")
        normed = sem("f_normed")
        stored = [sem(f"f_stored{i}") for i in range(2)]

        wu_v = w_up.rearrange("(k p) f -> p k f", p=P)
        wd_v = w_down.rearrange("(c k p) d -> c p k d", p=P, k=FT)
        block = ctx.enter_context(nc.Block())

        def walk(eng, step):
            def block_of(b):
                step(b, 0, 0)
                with eng.Fori(0, (NC - 4) // 2) as j:
                    step(b, 2 * j + 1, 1)
                    step(b, 2 * j + 2, 0)
                for c in range(NC - 3, NC):
                    step(b, c, c % 2)
            return block_of

        @block.sync
        def _(sp):
            def load_up(b, c):
                g = b * NC + c
                sp.wait_ge(wu_lo_done, g * FT)
                sp.dma_start(wu_raw[:], wu_v[:, :, bass.ds(c * C, C)]).then_inc(wu_loaded, 16)

            def load_down(b, c):
                g = b * NC + c
                if not (isinstance(g, int) and g == 0):
                    sp.wait_ge(wd_lo_done, g)
                sp.dma_start(wd_raw[:], wd_v[bass.ds(c, 1)].rearrange("a p k d -> (a p) k d")).then_inc(wd_loaded, 16)

            def tokens(b):
                return (NB - 1 - b) * T

            def load_h(b):
                for s in range(SBK):
                    cols = slice(tokens(b) + s * BANK, tokens(b) + (s + 1) * BANK)
                    for dst, src in ((h_hi, h_hi_dram), (h_lo, h_lo_dram)):
                        sp.dma_start(dst[:, :, s * BANK:(s + 1) * BANK].bitcast(F32),
                                     src[:, cols].rearrange("(k p) s -> p k s", p=P)).then_inc(h_loaded[s], 16)

            def load_acc(b, t):
                row = tokens(b) + t * P
                if b:
                    sp.wait_ge(normed, (b - 1) * ST + t + 1)
                sp.dma_start(acc[:, t], x_mid[row:row + P, :]).then_inc(acc_loaded, 16)

            def store(b, t):
                row = tokens(b) + t * P
                sp.wait_ge(normed, b * ST + t + 1)
                sp.dma_start(out[row:row + P, :], y[:, t % 2]).then_inc(stored[t % 2], 16)

            def step(b, c, parity):
                last = isinstance(c, int) and c == NC - 1
                if not last:
                    load_down(b, c + 1)
                    if isinstance(c, int) and c == NC - 2:
                        if b + 1 < NB:
                            load_up(b + 1, 0)
                    else:
                        load_up(b, c + 2)
                elif b + 1 < NB:
                    sp.wait_ge(upped, (b + 1) * NC * UPS)
                    load_h(b + 1)
                    load_up(b + 1, 1)
                    load_down(b + 1, 0)
                    for t in range(ST):
                        store(b, t)
                        load_acc(b + 1, t)
                else:
                    for t in range(ST):
                        store(b, t)

            load_down(0, 0)
            sp.dma_start(gain[:], norm_final.partition_broadcast(P)).then_inc(const_in, 16)
            load_up(0, 1)
            for t in range(ST):
                load_acc(0, t)
            for b in range(NB):
                walk(sp, step)(b)
            for i in range(2):
                sp.wait_ge(stored[i], 16 * NB * ST // 2)

        @block.gpsimd
        def _(pool):
            pool.wait_ge(mhalf_set, 1)
            with pool.Fori(0, NB * ST // 2) as i:
                for slot in range(2):
                    pool.wait_ge(squared, 2 * i + slot + 1)
                    nc.gpsimd.nop(nofuse=True)
                    nc.gpsimd.tensor_scalar(rstd[:, slot:slot + 1], ssum[:, slot:slot + 1], 1.0 / D, EPS,
                                            ALU.mult, ALU.add).then_inc(meaned, 1)
                    pool.wait_ge(meaned, 2 * i + slot + 1)
                    nc.gpsimd.tensor_tensor(rstd[:, slot:slot + 1], rstd[:, slot:slot + 1], mhalf[:],
                                            ALU.pow).then_inc(rooted, 1)

        @block.scalar
        def _(act):
            def split_up(g, parts=range(FT)):
                first = isinstance(g, int) and g == 0
                if not first:
                    act.wait_ge(wu_loaded, 16 * g)
                for f in parts:
                    cols = slice(f * P, (f + 1) * P)
                    if not first:
                        act.wait_ge(upped, (g - 1) * UPS + (f + 1) * SBK)
                    nc.scalar.activation(wu_hi[:, :, cols], wu_raw[:, :, cols], ACT.Copy).then_inc(wu_hi_done, 1)

            def split_down(g):
                act.wait_ge(wd_loaded, 16 * (g + 1))
                if not (isinstance(g, int) and g == 0):
                    act.wait_ge(downed, g * DOWNS)
                nc.scalar.activation(wd_hi[:], wd_raw[:], ACT.Copy).then_inc(wd_hi_done, 1)

            def activate(g, parity, n):
                q = g * UPS + n
                act.wait_ge(upped, q + 1)
                if not (isinstance(g, int) and q < 2):
                    act.wait_ge(sq_done, q - 1)
                nc.scalar.activation(r[:, n % 2], ps_u[n][:], ACT.Relu).then_inc(relu_done, 1)
                act.wait_ge(sq_done, q + 1)
                f, s = divmod(n, SBK)
                nc.scalar.activation(u_hi[parity][:, f, s * BANK:(s + 1) * BANK], sq[:, n % 2],
                                     ACT.Copy).then_inc(u_hi_done, 1)

            def square_sums(b):
                for t in range(ST):
                    act.wait_ge(added, (b * NC + NC - 1) * DOWNS + HALVES * (t + 1))
                    if t >= 2 or b:
                        act.wait_ge(stored[t % 2], 16 * ((b * ST + t) // 2))
                    nc.scalar.activation(y[:, t % 2], acc[:, t], ACT.Square,
                                         accum_out=ssum[:, t % 2:t % 2 + 1]).then_inc(squared, 1)

            def step(b, c, parity):
                g = b * NC + c
                if isinstance(c, int) and c == NC - 1:
                    split_down(g)
                    square_sums(b)
                    return
                if isinstance(c, int) and c == 0:
                    if b == 0:
                        split_up(0)
                    for n in range(UPS):
                        activate(g, 0, n)
                        if n % SBK == SBK - 1:
                            split_up(g + 1, (n // SBK,))
                activate(g + 1, 1 - parity, 0)
                split_down(g)
                for n in range(1, UPS):
                    activate(g + 1, 1 - parity, n)
                if not (isinstance(c, int) and c == NC - 2) or b + 1 < NB:
                    split_up(g + 2)

            for b in range(NB):
                walk(act, step)(b)

        @block.vector
        def _(dve):
            def split_up(g, parts=range(FT)):
                for f in parts:
                    cols = slice(f * P, (f + 1) * P)
                    dve.wait_ge(wu_hi_done, g * FT + f + 1)
                    nc.vector.tensor_tensor(wu_lo[:, :, cols], wu_raw[:, :, cols], wu_hi[:, :, cols].bitcast(F32),
                                            ALU.subtract).then_inc(wu_lo_done, 1)

            def split_down(g):
                dve.wait_ge(wd_hi_done, g + 1)
                nc.vector.tensor_tensor(wd_lo[:], wd_raw[:], wd_hi[:].bitcast(F32),
                                        ALU.subtract).then_inc(wd_lo_done, 1)

            def activate(g, parity, n):
                q = g * UPS + n
                f, s = divmod(n, SBK)
                cols = slice(s * BANK, (s + 1) * BANK)
                dve.wait_ge(relu_done, q + 1)
                nc.vector.tensor_tensor(sq[:, n % 2], r[:, n % 2], r[:, n % 2], ALU.mult).then_inc(sq_done, 1)
                dve.wait_ge(u_hi_done, q + 1)
                nc.vector.tensor_tensor(u_lo[parity][:, f, cols], sq[:, n % 2],
                                        u_hi[parity][:, f, cols].bitcast(F32), ALU.subtract).then_inc(u_lo_done, 1)

            def add(g, n):
                t, half = divmod(n, HALVES)
                cols = slice(half * BANK, (half + 1) * BANK)
                dve.wait_ge(downed, g * DOWNS + n + 1)
                nc.vector.tensor_tensor(acc[:, t, cols], acc[:, t, cols], ps_d[n % RING][:],
                                        ALU.add).then_inc(added, 1)

            def norm(b, t):
                dve.wait_ge(rooted, b * ST + t + 1)
                nc.vector.scalar_tensor_tensor(y[:, t % 2], acc[:, t], rstd[:, t % 2:t % 2 + 1], gain[:],
                                               ALU.mult, ALU.mult).then_inc(normed, 1)

            nc.vector.memset(mhalf[:], -0.5).then_inc(mhalf_set, 1)

            def step(b, c, parity):
                g = b * NC + c
                if isinstance(c, int) and c == NC - 1:
                    split_down(g)
                    if b == 0:
                        dve.wait_ge(const_in, 16)
                    for n in range(DOWNS):
                        add(g, n)
                        if n >= 2 * HALVES - 1 and n % HALVES == HALVES - 1:
                            norm(b, n // HALVES - 1)
                    norm(b, ST - 1)
                    return
                if isinstance(c, int) and c == 0:
                    if b == 0:
                        split_up(0)
                    for n in range(UPS):
                        activate(g, 0, n)
                        if n % SBK == SBK - 1:
                            split_up(g + 1, (n // SBK,))
                activate(g + 1, 1 - parity, 0)
                split_down(g)
                for n in range(1, UPS):
                    activate(g + 1, 1 - parity, n)
                if isinstance(c, int) and c == 0:
                    dve.wait_ge(acc_loaded, 16 * ST * (b + 1))
                for n in range(DOWNS):
                    if n == 4 and (not (isinstance(c, int) and c == NC - 2) or b + 1 < NB):
                        split_up(g + 2)
                    add(g, n)

            for b in range(NB):
                walk(dve, step)(b)

        @block.tensor
        def _(pe):
            def up(g, parity, b=None):
                for n in range(UPS):
                    f, s = divmod(n, SBK)
                    if s == 0:
                        pe.wait_ge(wu_lo_done, g * FT + f + 1)
                    if b and f == 0:
                        pe.wait_ge(h_loaded[s], 32 * b)
                    if not (isinstance(g, int) and g == 0):
                        pe.wait_ge(relu_done, (g - 1) * UPS + n + 1)
                    for k in range(DK):
                        for m, (w, h) in enumerate(((wu_hi, h_hi), (wu_hi, h_lo), (wu_lo, h_hi))):
                            last = nc.tensor.matmul(ps_u[n][:], w[:, k, f * P:(f + 1) * P],
                                                    h[:, k, s * BANK:(s + 1) * BANK],
                                                    start=(k == 0 and m == 0), stop=(k == DK - 1 and m == 2))
                    last.then_inc(upped, 1)

            def down(g, parity):
                pe.wait_ge(wd_lo_done, g + 1)
                pe.wait_ge(u_lo_done, (g + 1) * UPS)
                for n in range(DOWNS):
                    t, half = divmod(n, HALVES)
                    q = g * DOWNS + n
                    if not (isinstance(g, int) and q < RING):
                        pe.wait_ge(added, q - RING + 1)
                    for f in range(FT):
                        for m, (u, w) in enumerate(((u_hi, wd_hi), (u_hi, wd_lo), (u_lo, wd_hi))):
                            last = nc.tensor.matmul(ps_d[n % RING][:], u[parity][:, f, t * P:(t + 1) * P],
                                                    w[:, f, half * BANK:(half + 1) * BANK],
                                                    start=(f == 0 and m == 0), stop=(f == FT - 1 and m == 2))
                    last.then_inc(downed, 1)

            def step(b, c, parity):
                g = b * NC + c
                if isinstance(c, int) and c == 0:
                    up(g, 0, b)
                if not (isinstance(c, int) and c == NC - 1):
                    up(g + 1, 1 - parity)
                down(g, parity)

            for b in range(NB):
                walk(pe, step)(b)


def out_and_mlp(nc, o_main, o_rest, rsum_inv, w_out, x, norm_mlp, w_up, w_down, norm_final, ident,
                x_mid, h_hi_dram, h_lo_dram, out):
    DK = x.shape[1] // P
    with ExitStack() as ctx:
        sb, _, _ = scopes(nc, ctx)
        h_hi = sb("h_hi_kept", [P, DK, MLP_TOKENS], F32R)
        h_lo = sb("h_lo_kept", [P, DK, MLP_TOKENS], F32R)
        wu_raw = sb("wu_raw_kept", [P, DK, MLP_CHUNK])
        mix_out(nc, o_main, o_rest, rsum_inv, w_out, x, norm_mlp, w_up, ident, h_hi, h_lo, wu_raw,
                x_mid, h_hi_dram, h_lo_dram)
        mlp(nc, x_mid, h_hi, h_lo, wu_raw, h_hi_dram, h_lo_dram, w_up, w_down, norm_final, out)


def hybrid_block(nc, x, norm_mix, w_in, b_forget, sinks, w_out, norm_mlp, w_up, w_down, norm_final,
                 ident, causal, alibi, out):
    x, out = (a.rearrange("b s d -> (b s) d") for a in (x, out))
    w_in, w_out, w_up, w_down = (w.rearrange("l a b -> (l a) b") for w in (w_in, w_out, w_up, w_down))
    S, D = x.shape
    E = w_out.shape[0]
    rows = -(-w_in.shape[1] // P) * P

    def scratch(name, *shape):
        return nc.dram_tensor(name, shape, F32).ap()

    proj_hi, proj_lo = scratch("proj_hi", rows, S), scratch("proj_lo", rows, S)
    decay = scratch("decay", FOX_HEADS, S)
    o_main, o_rest = scratch("o_main", E, S), scratch("o_rest", E, S)
    rsum_inv = scratch("rsum_inv", SWA_HEADS + FOX_HEADS, S)
    x_mid = scratch("x_mid", S, D)
    h_hi, h_lo = scratch("h_hi", D, S), scratch("h_lo", D, S)

    project(nc, x, norm_mix, w_in, b_forget, ident, proj_hi, proj_lo, decay)
    attend(nc, proj_hi, proj_lo, sinks, ident, causal, alibi, decay, o_main, o_rest, rsum_inv)
    out_and_mlp(nc, o_main, o_rest, rsum_inv, w_out, x, norm_mlp, w_up, w_down, norm_final, ident,
                x_mid, h_hi, h_lo, out)


_INS = ["x", "norm_mix", "w_in", "b_forget", "sinks", "w_out", "norm_mlp", "w_up", "w_down", "norm_final"]


def kernel(**inputs):
    import numpy as np
    import concourse.bacc as bacc
    from concourse.bass_utils import run_bass_kernel_spmd

    nc = bacc.Bacc("TRN2", target_bir_lowering=False, num_devices=1)
    arrays = {name: np.ascontiguousarray(inputs[name]) for name in _INS}
    causal, alibi = tables()
    arrays |= {"ident": np.eye(P, dtype=np.float32), "causal": causal, "alibi": alibi}
    args = [nc.dram_tensor(f"in_{name}", a.shape, mybir.dt.from_np(a.dtype), kind="ExternalInput").ap()
            for name, a in arrays.items()]
    shape = arrays["x"].shape
    out = nc.dram_tensor("out_0", shape, F32, kind="ExternalOutput").ap()
    hybrid_block(nc, *args, out)
    r = run_bass_kernel_spmd(nc, [{f"in_{name}": a for name, a in arrays.items()}], core_ids=[0])
    return r.results[0]["out_0"]
```
